# Optimizing a Trainium2 kernel written in Bass

```python
import math
import jax, jax.numpy as jnp
from jax import lax
import numpy as np

D_MODEL = 1024
BATCH = 1
SEQ = 256
DEPTH = 2

PLE_DIM = 256
N_NORMS = 6
EPS = 1e-6
D_RNN = 1024
N_RNN_BLOCKS = 16
RNN_BLOCK = D_RNN // N_RNN_BLOCKS
CONV_WIDTH = 4
LRU_C = 8.0
N_DIFF_HEADS = 8
DIFF_HEAD_DIM = 64
DIFF_V_DIM = 2 * DIFF_HEAD_DIM
D_QK = N_DIFF_HEADS * 2 * DIFF_HEAD_DIM
D_ATTN = N_DIFF_HEADS * DIFF_V_DIM
ROPE_THETA = 10000.0
Q_BLOCK = 128
D_FF = 3584
N_EXPERTS = 8
TOP_K = 2
N_DENSE_LAYERS = (DEPTH + 1) // 2
N_MOE_LAYERS = DEPTH // 2
D_IN = 2 * D_RNN + 2 * D_QK + D_ATTN + 2 * D_MODEL
SPLIT_POINTS = (D_RNN, 2 * D_RNN, 2 * D_RNN + D_QK, 2 * D_RNN + 2 * D_QK,
                2 * D_RNN + 2 * D_QK + D_ATTN, 2 * D_RNN + 2 * D_QK + D_ATTN + D_MODEL)

kernel_name = 'hybrid_rglru_diffattn_moe_block'

def rmsnorm(x, g):
    xf = x.astype(jnp.float32)
    xf = xf * lax.rsqrt(jnp.mean(xf * xf, axis=-1, keepdims=True) + EPS)
    return (xf * g.astype(jnp.float32)).astype(x.dtype)

def rope_tables(positions):
    inv_freq = ROPE_THETA ** (-jnp.arange(0, DIFF_HEAD_DIM, 2, dtype=jnp.float32) / DIFF_HEAD_DIM)
    ang = positions.astype(jnp.float32)[..., None] * inv_freq
    ang = jnp.concatenate([ang, ang], axis=-1)
    return jnp.cos(ang), jnp.sin(ang)

def apply_rope(t, cos, sin):
    half = DIFF_HEAD_DIM // 2
    tf = t.astype(jnp.float32)
    rot = jnp.concatenate([-tf[..., half:], tf[..., :half]], axis=-1)
    c = cos[:, :, None, None, :]
    s = sin[:, :, None, None, :]
    return (tf * c + rot * s).astype(t.dtype)

def causal_depthwise_conv(u, w, b):
    y = lax.conv_general_dilated(u, w[:, None, :].astype(u.dtype), window_strides=(1,),
                                 padding=[(CONV_WIDTH - 1, 0)],
                                 dimension_numbers=('NWC', 'WIO', 'NWC'),
                                 feature_group_count=D_RNN)
    return y + b

def rg_lru(u, w_a, b_a, w_x, b_x, lam):
    bsz, seq, _ = u.shape
    ub = u.reshape(bsz, seq, N_RNN_BLOCKS, RNN_BLOCK)
    r = jax.nn.sigmoid(jnp.einsum('bsnc,ncd->bsnd', ub, w_a).reshape(bsz, seq, D_RNN) + b_a)
    i_gate = jax.nn.sigmoid(jnp.einsum('bsnc,ncd->bsnd', ub, w_x).reshape(bsz, seq, D_RNN) + b_x)
    log_a = -LRU_C * r.astype(jnp.float32) * jax.nn.softplus(-lam.astype(jnp.float32))
    a = jnp.exp(log_a)
    beta = jnp.sqrt(-jnp.expm1(2.0 * log_a))
    b = beta * (i_gate * u).astype(jnp.float32)

    def combine(left, right):
        a_l, b_l = left
        a_r, b_r = right
        return a_l * a_r, a_r * b_l + b_r

    _, h = lax.associative_scan(combine, (a, b), axis=1)
    return h.astype(u.dtype)

def diff_attention(q, k, v, lam, lambda_init, g_sub):
    seq = q.shape[2]
    scale = DIFF_HEAD_DIM ** -0.5
    outs = []
    for j in range(seq // Q_BLOCK):
        q0 = j * Q_BLOCK
        kv_len = q0 + Q_BLOCK
        s = jnp.einsum('bhqmd,bhkmd->bhmqk', q[:, :, q0:kv_len], k[:, :, :kv_len]).astype(jnp.float32) * scale
        causal = (q0 + jnp.arange(Q_BLOCK))[:, None] >= jnp.arange(kv_len)[None, :]
        s = jnp.where(causal, s, -1e30)
        prob = jax.nn.softmax(s, axis=-1)
        w = prob[:, :, 0] - lam * prob[:, :, 1]
        outs.append(jnp.einsum('bhqk,bhkd->bhqd', w.astype(v.dtype), v[:, :, :kv_len]))
    o = jnp.concatenate(outs, axis=2)
    o = rmsnorm(o, g_sub) * (1.0 - lambda_init)
    bsz = o.shape[0]
    return o.transpose(0, 2, 1, 3).reshape(bsz, seq, D_ATTN)

def swiglu(h, w_gate, w_up, w_down):
    return (jax.nn.silu(h @ w_gate) * (h @ w_up)) @ w_down

def moe_swiglu(h, router_w, w_gate, w_up, w_down):
    bsz, seq, d = h.shape
    t = h.reshape(bsz * seq, d)
    logits = (t @ router_w).astype(jnp.float32)
    top_val, top_idx = lax.top_k(logits, TOP_K)
    top_w = jax.nn.softmax(top_val, axis=-1)
    combine = jnp.sum(jax.nn.one_hot(top_idx, N_EXPERTS, dtype=jnp.float32) * top_w[..., None], axis=1)
    out = jnp.zeros_like(t)
    for e in range(N_EXPERTS):
        out = out + combine[:, e:e + 1].astype(t.dtype) * swiglu(t, w_gate[e], w_up[e], w_down[e])
    return out.reshape(bsz, seq, d)

def setup_inputs(seed: int = 0) -> dict:
    key = jax.random.key(seed)
    ks = jax.random.split(key, 28)
    f32 = jnp.float32

    def nrm(k, shape, scale):
        return jax.random.normal(k, shape, f32) * scale

    x = nrm(ks[0], (BATCH, SEQ, D_MODEL), 1.0)
    p = nrm(ks[1], (DEPTH, BATCH, SEQ, PLE_DIM), 1.0)
    offsets = jax.random.randint(ks[2], (BATCH, 1), 0, 1024, dtype=jnp.int32)
    positions = offsets + jnp.arange(SEQ, dtype=jnp.int32)[None, :]
    norm_g = 1.0 + nrm(ks[3], (DEPTH, N_NORMS, D_MODEL), 0.01)
    w_in = nrm(ks[4], (DEPTH, D_MODEL, D_IN), D_MODEL ** -0.5)
    conv_w = nrm(ks[5], (DEPTH, CONV_WIDTH, D_RNN), CONV_WIDTH ** -0.5)
    conv_b = nrm(ks[6], (DEPTH, D_RNN), 0.01)
    lru_wa = nrm(ks[7], (DEPTH, N_RNN_BLOCKS, RNN_BLOCK, RNN_BLOCK), RNN_BLOCK ** -0.5)
    lru_ba = nrm(ks[8], (DEPTH, D_RNN), 0.01)
    lru_wx = nrm(ks[9], (DEPTH, N_RNN_BLOCKS, RNN_BLOCK, RNN_BLOCK), RNN_BLOCK ** -0.5)
    lru_bx = nrm(ks[10], (DEPTH, D_RNN), 0.01)
    a0 = jax.random.uniform(ks[11], (DEPTH, D_RNN), f32, 0.9, 0.999)
    a_root = a0 ** (1.0 / LRU_C)
    lru_lam = jnp.log(a_root) - jnp.log1p(-a_root)
    diff_lambda = nrm(ks[12], (DEPTH, 4, DIFF_HEAD_DIM), 0.1)
    subln_g = 1.0 + nrm(ks[13], (DEPTH, DIFF_V_DIM), 0.01)
    w_proj_a = nrm(ks[14], (DEPTH, D_RNN, D_MODEL), D_RNN ** -0.5)
    w_proj_b = nrm(ks[15], (DEPTH, D_ATTN, D_MODEL), D_ATTN ** -0.5)
    w_out = nrm(ks[16], (DEPTH, D_MODEL, D_MODEL), D_MODEL ** -0.5)
    ffn_w_gate = nrm(ks[17], (N_DENSE_LAYERS, D_MODEL, D_FF), D_MODEL ** -0.5)
    ffn_w_up = nrm(ks[18], (N_DENSE_LAYERS, D_MODEL, D_FF), D_MODEL ** -0.5)
    ffn_w_down = nrm(ks[19], (N_DENSE_LAYERS, D_FF, D_MODEL), D_FF ** -0.5)
    router_w = nrm(ks[20], (N_MOE_LAYERS, D_MODEL, N_EXPERTS), D_MODEL ** -0.5)
    moe_w_gate = nrm(ks[21], (N_MOE_LAYERS, N_EXPERTS, D_MODEL, D_FF), D_MODEL ** -0.5)
    moe_w_up = nrm(ks[22], (N_MOE_LAYERS, N_EXPERTS, D_MODEL, D_FF), D_MODEL ** -0.5)
    moe_w_down = nrm(ks[23], (N_MOE_LAYERS, N_EXPERTS, D_FF, D_MODEL), D_FF ** -0.5)
    ple_w_proj = nrm(ks[24], (DEPTH, PLE_DIM, D_MODEL), PLE_DIM ** -0.5)
    ple_w_gate = nrm(ks[25], (DEPTH, D_MODEL, D_MODEL), D_MODEL ** -0.5)
    return {'x': x, 'p': p, 'positions': positions, 'norm_g': norm_g, 'w_in': w_in,
            'conv_w': conv_w, 'conv_b': conv_b, 'lru_wa': lru_wa, 'lru_ba': lru_ba,
            'lru_wx': lru_wx, 'lru_bx': lru_bx, 'lru_lam': lru_lam,
            'diff_lambda': diff_lambda, 'subln_g': subln_g, 'w_proj_a': w_proj_a,
            'w_proj_b': w_proj_b, 'w_out': w_out, 'ffn_w_gate': ffn_w_gate,
            'ffn_w_up': ffn_w_up, 'ffn_w_down': ffn_w_down, 'router_w': router_w,
            'moe_w_gate': moe_w_gate, 'moe_w_up': moe_w_up, 'moe_w_down': moe_w_down,
            'ple_w_proj': ple_w_proj, 'ple_w_gate': ple_w_gate}

def reference(x, p, positions, norm_g, w_in, conv_w, conv_b, lru_wa, lru_ba, lru_wx, lru_bx,
              lru_lam, diff_lambda, subln_g, w_proj_a, w_proj_b, w_out, ffn_w_gate, ffn_w_up,
              ffn_w_down, router_w, moe_w_gate, moe_w_up, moe_w_down, ple_w_proj, ple_w_gate):
    bsz, seq, _ = x.shape
    cos, sin = rope_tables(positions)
    for i in range(DEPTH):
        lambda_init = 0.8 - 0.6 * math.exp(-0.3 * i)
        h = rmsnorm(x, norm_g[i, 0])
        proj = h @ w_in[i]
        rnn_gate, rnn_in, q, k, v, g_a, g_b = jnp.split(proj, SPLIT_POINTS, axis=-1)
        u = causal_depthwise_conv(rnn_in, conv_w[i], conv_b[i])
        y_a = rg_lru(u, lru_wa[i], lru_ba[i], lru_wx[i], lru_bx[i], lru_lam[i]) * jax.nn.gelu(rnn_gate)
        q = apply_rope(q.reshape(bsz, seq, N_DIFF_HEADS, 2, DIFF_HEAD_DIM), cos, sin).transpose(0, 2, 1, 3, 4)
        k = apply_rope(k.reshape(bsz, seq, N_DIFF_HEADS, 2, DIFF_HEAD_DIM), cos, sin).transpose(0, 2, 1, 3, 4)
        v = v.reshape(bsz, seq, N_DIFF_HEADS, DIFF_V_DIM).transpose(0, 2, 1, 3)
        lq1, lk1, lq2, lk2 = diff_lambda[i].astype(jnp.float32)
        lam = jnp.exp(jnp.sum(lq1 * lk1)) - jnp.exp(jnp.sum(lq2 * lk2)) + lambda_init
        y_b = diff_attention(q, k, v, lam, lambda_init, subln_g[i])
        merged = jax.nn.sigmoid(g_a) * (y_a @ w_proj_a[i]) + jax.nn.sigmoid(g_b) * (y_b @ w_proj_b[i])
        x = x + rmsnorm(merged @ w_out[i], norm_g[i, 1])
        h = rmsnorm(x, norm_g[i, 2])
        if i % 2 == 0:
            f = swiglu(h, ffn_w_gate[i // 2], ffn_w_up[i // 2], ffn_w_down[i // 2])
        else:
            f = moe_swiglu(h, router_w[i // 2], moe_w_gate[i // 2], moe_w_up[i // 2], moe_w_down[i // 2])
        x = x + rmsnorm(f, norm_g[i, 3])
        gate = jax.nn.sigmoid(rmsnorm(x, norm_g[i, 4]) @ ple_w_gate[i])
        x = x + rmsnorm(gate * (p[i] @ ple_w_proj[i]), norm_g[i, 5])
    return x


_drawn_inputs = setup_inputs


def setup_inputs(seed=0):
    import zlib

    import numpy as np

    out = dict(_drawn_inputs(seed))
    spreads = {}
    factors = {'lru_ba': 28.878, 'lru_bx': 28.735}
    for name, (base, spread) in spreads.items():
        noise = np.random.default_rng([zlib.crc32(name.encode()), seed]).standard_normal(out[name].shape)
        drawn = base * np.exp(spread * noise) if base else spread * noise
        out[name] = __import__('jax').numpy.asarray(drawn.astype(out[name].dtype))
    for name, factor in factors.items():
        out[name] = (out[name] * factor).astype(out[name].dtype)
    return out
```

```python
import math
from contextlib import ExitStack

import numpy as np

import concourse.bass as bass
from concourse import mybir

ALU = mybir.AluOpType
ACT = mybir.ActivationFunctionType
AX = mybir.AxisListType
F32 = mybir.dt.float32
F32R = mybir.dt.float32r
I32 = mybir.dt.int32

P = 128
D = 1024
SEQ = 256
DEPTH = 2
KT = D // P
BLK = SEQ // P
PLE = 256
PKT = PLE // P
N_NORMS = 6
EPS = 1e-6
HEADS = 8
HD = 64
D_FF = 3584
FT = D_FF // P
EXPERTS = 8
NEG = -1e30
TOKENS = P
MAX_EXTRA = 3
MAX_JOBS = EXPERTS + MAX_EXTRA

CH = 2048
RAW = 6
HC = CH // 2
SPL = 3
MIX = 40
GU = 28
FFN = 42
PLEC = 5
BASE = (0, MIX + FFN + PLEC)
FFN0 = MIX
PLE0 = MIX + FFN
MOE0 = BASE[1] + MIX
GROUP = (1, 0, 2, 3, 4, 5, 6)
N_LD = 12
U7 = 9
SCATTER = (1, 4, 8, 12)
TURN_W = 16
GATHER = (31, 33, 35, 37)
assert FFN % RAW == 0 and FFN % SPL == 0


def bass_hybrid_rglru_diffattn_moe(nc, x, p, positions, norm_g, w_in, conv_w, conv_b, lru_wa, lru_ba, lru_wx,
                                   lru_bx, lru_lam, diff_lambda, subln_g, w_proj_a, w_proj_b, w_out, ffn_w_gate,
                                   ffn_w_up, ffn_w_down, router_w, moe_w_gate, moe_w_up, moe_w_down, ple_w_proj,
                                   ple_w_gate, inv_freq, out):
    ctx = ExitStack()
    with ctx:
        base0 = 16512
        cursor = [base0]

        def at(name, off, shape, dt=F32):
            return nc.alloc_sbuf_tensor_at(name, shape, dt, offset=off)

        def keep(name, shape, dt=F32):
            off = cursor[0]
            size = 4 * int(np.prod(shape[1:]))
            cursor[0] = off + (size + 31) // 32 * 32
            return at(name, off, shape, dt)

        raw = [keep(f"raw{i}", [P, CH]) for i in range(RAW)]
        whi = [keep(f"whi{i}", [P, CH], F32R) for i in range(SPL)]
        wlo = [keep(f"wlo{i}", [P, CH], F32R) for i in range(SPL)]
        XF = keep("XF", [P, KT, SEQ])
        PF = keep("PF", [P, DEPTH, PKT, SEQ])
        IDENT = keep("IDENT", [P, P])
        SWAP = keep("SWAP", [P, P])
        ONES = keep("ONES", [P, P])
        BEFORE = keep("BEFORE", [P, P])
        IOTA = keep("IOTA", [P, P])
        MASK = keep("MASK", [P, SEQ])
        COS = keep("COS", [P, SEQ])
        SIN = keep("SIN", [P, SEQ])
        V1 = keep("V1", [P, 98])
        V2 = keep("V2", [P, P])
        SPLAM = keep("SPLAM", [P, DEPTH * KT])
        GSUB = keep("GSUB", [P, DEPTH])
        NLAM = keep("NLAM", [P, DEPTH])
        EPSC = keep("EPSC", [P, 1])
        RW = keep("RW", [P, KT, EXPERTS])
        STD = keep("STD", [P, SEQ])
        RINV = keep("RINV", [P, SEQ])
        SM = keep("SM", [P, 160])
        RT = keep("RT", [P, 18, BLK, EXPERTS])
        AMX = keep("AMX", [P, 2, 4])
        ASUM = keep("ASUM", [P, 2, 4])
        AR = keep("AR", [P, 2, 4])
        JR = keep("JR", [P, BLK, MAX_JOBS + 1])
        JC = keep("JC", [P, BLK, MAX_JOBS + 1])
        JINFO = keep("JINFO", [P, 4], I32)
        arena = cursor[0]
        KB = 1024
        end = 229344

        a0 = arena
        HH = at("HH", a0, [P, KT, SEQ], F32R)
        HL = at("HL", a0 + 8 * KB, [P, KT, SEQ], F32R)
        o_rin = a0 + 16 * KB
        RIN = at("RIN", o_rin, [P, KT, SEQ + 3])
        o_bd = o_rin + 8 * KB + 128
        BD = at("BD", o_bd, [P, 2, KT, P])
        YAH = at("YAH", o_rin, [P, KT, SEQ], F32R)
        YAL = at("YAL", o_bd, [P, KT, SEQ], F32R)
        o_rt = o_bd + 8 * KB
        U = at("U", o_rt, [P, 4, SEQ])
        T2 = at("T2", o_rt + 4 * KB, [P, 4, SEQ])
        IG = at("IG", o_rt + 8 * KB, [P, 4, SEQ])
        SQ = at("SQ", o_rt + 12 * KB, [P, 4, SEQ])
        SC = at("SC", o_rt, [P, 2, 3 * SEQ])
        WT = at("WT", o_rt + 6 * KB, [P, 2, 3 * P])
        OSQ = at("OSQ", o_rt + 9 * KB, [P, 2, SEQ])
        o_gel = o_rt + 16 * KB
        GEL = at("GEL", o_gel, [P, KT, SEQ])
        SGB = at("SGB", o_gel, [P, KT, SEQ])
        o_q = o_gel + 8 * KB
        Q = at("Q", o_q, [P, KT, SEQ])
        K = at("K", o_q + 8 * KB, [P, KT, SEQ])
        V = at("V", o_q + 16 * KB, [P, BLK, D])
        o_sga = o_q + 24 * KB
        SGA = at("SGA", o_sga, [P, KT, SEQ])
        QT = at("QT", o_sga, [P, 2, 2, SEQ])
        QS = at("QS", o_sga + 4 * KB, [P, 2, SEQ])
        top = o_sga + 8 * KB
        assert top <= end, (top, end)
        OALL, MSALL = Q, K
        YBH, YBL = HH, HL
        Z, ZSQ, HF = Q, K, at("HF", o_q + 16 * KB, [P, KT, SEQ])

        FH = at("FH", a0 + 16 * KB, [P, FT, SEQ], F32R)
        FL = at("FL", a0 + 44 * KB, [P, FT, SEQ], F32R)
        FS = at("FS", a0 + 72 * KB, [P, 2, 512])
        FA = at("FA", a0 + 76 * KB, [P, 2, 512])

        PP = at("PP", o_rt, [P, KT, SEQ])
        PG = at("PG", o_rt + 8 * KB, [P, 2, 512])
        PHI = at("PHI", o_rt + 12 * KB, [P, PKT, SEQ], F32R)
        PLO = at("PLO", o_rt + 14 * KB, [P, PKT, SEQ], F32R)

        HTH = at("HTH", a0, [P, BLK, D], F32R)
        HTL = at("HTL", a0 + 8 * KB, [P, BLK, D], F32R)
        XGH = at("XGH", a0 + 16 * KB, [P, KT, TOKENS], F32R)
        XGL = at("XGL", a0 + 20 * KB, [P, KT, TOKENS], F32R)
        ATH = at("ATH", a0 + 24 * KB, [P, FT, TOKENS], F32R)
        ATL = at("ATL", a0 + 38 * KB, [P, FT, TOKENS], F32R)
        o_m = a0 + 52 * KB
        FACC = at("FACC", o_q, [P, KT, SEQ])
        o_m = o_sga
        MS = at("MS", a0 + 52 * KB, [P, 2, 512])
        DSEL = at("DSEL", o_m, [P, BLK, TOKENS], F32R)
        DC = at("DC", o_m + 1 * KB, [P, BLK, TOKENS])
        S = at("S", o_m + 2 * KB, [P, SEQ])
        MA = at("MA", o_q + 8 * KB, [P, 2, 512])
        Y = at("Y", o_m + 4 * KB, [P, D])
        assert a0 + 56 * KB <= o_q

        XT = at("XT", o_q, [P, BLK, D])
        PT = at("PT", o_q + 8 * KB, [P, DEPTH * BLK, PLE])
        R1 = at("R1", o_q + 12 * KB, [98, P])
        R2 = at("R2", o_q + 13 * KB, [P, P])
        DL = at("DL", o_q + 14 * KB, [P, DEPTH * 4, HD])
        POSI = at("POSI", o_sga, [P, SEQ], I32)
        POSF = at("POSF", o_sga + KB, [P, SEQ])
        TT = at("TT", o_sga + 2 * KB, [P, 4, SEQ])
        IFR = at("IFR", o_sga + 6 * KB, [P, 1])
        OT = at("OT", a0, [P, BLK, D])

        B = [ctx.enter_context(nc.psum_tensor(f"bank{i}", [P, 512], F32)) for i in range(8)]

        def sem(name):
            return ctx.enter_context(nc.semaphore(name))

        s_w = [sem(f"s_w{i}") for i in range(RAW)]
        s_hi = sem("s_hi")
        s_lo = sem("s_lo")
        s_pe = sem("s_pe")
        s_ld = sem("s_ld")
        s_ldx = sem("s_ldx")
        s_bd = sem("s_bd")
        s_bdz = sem("s_bdz")
        s_pool = sem("s_pool")
        s_ac = sem("s_ac")
        s_dc = sem("s_dc")
        s_tp = sem("s_tp")
        s_tc = sem("s_tc")
        s_r0 = sem("s_r0")
        s_r1 = sem("s_r1")
        s_c0 = sem("s_c0")
        s_c1 = sem("s_c1")
        s_c2 = sem("s_c2")
        s_eva = sem("s_eva")
        s_evd = sem("s_evd")
        s_u = sem("s_u")
        s_gt = sem("s_gt")
        s_ga = sem("s_ga")
        s_sq = sem("s_sq")
        s_rh = sem("s_rh")
        s_y = sem("s_y")
        s_yh = sem("s_yh")
        s_ya = sem("s_ya")
        s_qt = sem("s_qt")
        s_qs = sem("s_qs")
        s_qr = sem("s_qr")
        s_sc = sem("s_sc")
        s_mx = sem("s_mx")
        s_ex = sem("s_ex")
        s_df = sem("s_df")
        s_wt = sem("s_wt")
        s_wc = sem("s_wc")
        s_o = sem("s_o")
        s_oc = sem("s_oc")
        s_om = sem("s_om")
        s_oe = sem("s_oe")
        s_os = sem("s_os")
        s_yf = sem("s_yf")
        s_ybh = sem("s_ybh")
        s_yb = sem("s_yb")
        s_m = sem("s_m")
        s_mh = sem("s_mh")
        s_ml = sem("s_ml")
        s_zq = sem("s_zq")
        s_zp = sem("s_zp")
        s_zm = sem("s_zm")
        s_zs = sem("s_zs")
        s_xn = sem("s_xn")
        s_xq = sem("s_xq")
        s_xm = sem("s_xm")
        s_xs = sem("s_xs")
        s_hf = sem("s_hf")
        s_hh = sem("s_hh")
        s_hl = sem("s_hl")
        f_s = sem("f_s")
        f_a = sem("f_a")
        f_h = sem("f_h")
        f_l = sem("f_l")
        s_ph = sem("s_ph")
        s_pl = sem("s_pl")
        s_pp = sem("s_pp")
        s_pg = sem("s_pg")
        r_lg = sem("r_lg")
        r_d = sem("r_d")
        r_e = sem("r_e")
        r_sel = sem("r_sel")
        r_rk = sem("r_rk")
        r_j = sem("r_j")
        r_tp = sem("r_tp")
        r_th = sem("r_th")
        r_tl = sem("r_tl")
        m_z = sem("m_z")
        m_s = sem("m_s")
        m_a = sem("m_a")
        m_t = sem("m_t")
        m_th = sem("m_th")
        m_tl = sem("m_tl")
        m_d = sem("m_d")
        m_dc = sem("m_dc")
        m_p7 = sem("m_p7")
        m_b7 = sem("m_b7")
        m_y0 = sem("m_y0")
        m_y1 = sem("m_y1")
        s_ot = sem("s_ot")
        s_oo = sem("s_oo")
        s_out = sem("s_out")

        def eva(layer, c):
            return 32 * layer + (c + 1 if c < 28 else c - 36 + 29)

        def evd(layer, c):
            return 8 * layer + c - 28 + 1

        def rows(w):
            return w.rearrange("(k p) n -> p k n", p=P)

        block = ctx.enter_context(nc.Block())

        @block.sync
        def _(sp):
            def load(b, jobs, src, k):
                if isinstance(jobs, int) and b + FFN * jobs < RAW:
                    pass
                else:
                    sp.wait_ge(s_lo, 2 * (b - RAW + 1) + 2 * FFN * jobs)
                sp.dma_start(raw[b % RAW][:, :].rearrange("p (k n) -> p k n", k=k), src).then_inc(s_w[b % RAW], 16)

            def mixer(layer):
                b = BASE[layer]
                wi = rows(w_in[layer])
                for c in range(28):
                    col = GROUP[c // 4] * D + (c % 4) * 256
                    load(b + c, 0, wi[:, :, col:col + 256], 8)
                for n, w in enumerate((w_proj_a, w_proj_b, w_out)):
                    for c in range(4):
                        load(b + 28 + 4 * n + c, 0, rows(w[layer])[:, :, 256 * c:256 * c + 256], 8)

            def embed(b, jobs, layer):
                load(b, jobs, rows(ple_w_proj[layer]), 2)
                for c in range(4):
                    load(b + 1 + c, jobs, rows(ple_w_gate[layer])[:, :, 256 * c:256 * c + 256], 8)

            def expert(jobs, e):
                wg, wu, wd = (w[0, bass.ds(e, 1)].rearrange("a (k p) n -> p (a k) n", p=P)
                              for w in (moe_w_gate, moe_w_up, moe_w_down))
                for f in range(7):
                    for n, w in enumerate((wg, wu)):
                        for h in range(2):
                            load(MOE0 + 4 * f + 2 * n + h, jobs, w[:, 4 * h:4 * h + 4, 512 * f:512 * f + 512], 4)
                for d in range(14):
                    load(MOE0 + GU + d, jobs, wd[:, 2 * d:2 * d + 2, :], 2)

            mixer(0)
            gate, up = rows(ffn_w_gate[0]), rows(ffn_w_up[0])
            with sp.Fori(0, 2) as it:
                for s in range(6):
                    for n, w in enumerate((gate, up)):
                        b = FFN0 + 2 * s + n
                        sp.wait_ge(s_lo, 2 * (b - RAW + 1) + 24 * it)
                        sp.dma_start(raw[b % RAW][:, :].rearrange("p (k n) -> p k n", k=8),
                                     w[:, :, bass.ds(it * 1536 + 256 * s, 256)]).then_inc(s_w[b % RAW], 16)
            for s in range(12, 14):
                load(FFN0 + 2 * s, 0, gate[:, :, 256 * s:256 * s + 256], 8)
                load(FFN0 + 2 * s + 1, 0, up[:, :, 256 * s:256 * s + 256], 8)
            for d in range(14):
                load(FFN0 + GU + d, 0, rows(ffn_w_down[0])[:, 2 * d:2 * d + 2, :], 2)
            embed(PLE0, 0, 0)
            mixer(1)
            with sp.Fori(0, EXPERTS) as j:
                expert(j, j)
            sp.wait_ge(r_j, 1)
            jobs = sp.value_load(JINFO[0:1, 0:1], min_val=EXPERTS, max_val=MAX_JOBS)
            for extra in range(MAX_EXTRA):
                with sp.If(jobs > EXPERTS + extra):
                    e = sp.value_load(JINFO[0:1, 1 + extra:2 + extra], min_val=0, max_val=EXPERTS - 1)
                    expert(EXPERTS + extra, e)
            embed(MOE0, jobs, 1)
            for blk in range(BLK):
                sp.wait_ge(s_oo, 2 * blk + 2)
                sp.dma_start(out[0, P * blk:P * blk + P, :], OT[:, blk, :]).then_inc(s_out, 16)
            sp.wait_ge(s_out, 16 * BLK)

        @block.gpsimd
        def _(pool):
            pool.memset(IDENT[:, :], 0.0).then_inc(s_pool, 1)
            pool.memset(SWAP[:, :], 0.0).then_inc(s_pool, 1)
            pool.memset(ONES[:, :], 1.0).then_inc(s_pool, 1)
            pool.memset(BEFORE[:, :], 1.0).then_inc(s_pool, 1)
            pool.memset(MASK[:, :], 0.0).then_inc(s_pool, 1)
            pool.memset(EPSC[:, :], EPS).then_inc(s_pool, 1)
            pool.memset(RIN[:, :, 0:3], 0.0).then_inc(s_pool, 1)
            pool.memset(JR[:, :, EXPERTS:], -1.0).then_inc(s_pool, 1)
            pool.memset(JC[:, :, EXPERTS:], 0.0).then_inc(s_pool, 1)
            pool.memset(BD[:, :, :, :], 0.0).then_inc(s_bdz, 1)
            pool.iota(IOTA[:, :], [[1, P]], base=0, channel_multiplier=0,
                      allow_small_or_imprecise_dtypes=True).then_inc(s_pool, 1)
            pool.wait_ge(s_pool, 10)
            pool.affine_select(out=IDENT[:, :], in_=IDENT[:, :], compare_op=ALU.not_equal, fill=1.0, base=0,
                               pattern=[[-1, P]], channel_multiplier=1).then_inc(s_pool, 1)
            sw = SWAP[:, :].rearrange("p (g h j) -> p g h j", g=2, h=2)
            pool.affine_select(out=sw[:, :, 0, :], in_=sw[:, :, 0, :], compare_op=ALU.not_equal, fill=-1.0, base=-32,
                               pattern=[[-64, 2], [-1, 32]], channel_multiplier=1).then_inc(s_pool, 1)
            pool.affine_select(out=sw[:, :, 1, :], in_=sw[:, :, 1, :], compare_op=ALU.not_equal, fill=1.0, base=0,
                               pattern=[[-64, 2], [-1, 32]], channel_multiplier=1).then_inc(s_pool, 1)
            pool.affine_select(out=BEFORE[:, :], in_=BEFORE[:, :], compare_op=ALU.is_gt, fill=0.0, base=0,
                               pattern=[[1, P]], channel_multiplier=-1).then_inc(s_pool, 1)
            pool.affine_select(out=MASK[:, P:SEQ], in_=MASK[:, P:SEQ], compare_op=ALU.is_ge, fill=NEG, base=0,
                               pattern=[[-1, P]], channel_multiplier=1).then_inc(s_pool, 1)

            def gates(layer):
                for kind, w in enumerate((lru_wa, lru_wx)):
                    pairs = w[layer].rearrange("(t h) c d -> h c t d", h=2)
                    for h in range(2):
                        pool.dma_start(BD[HD * h:HD * h + HD, kind, :, HD * h:HD * h + HD], pairs[h]).then_inc(s_bd, 16)

            pool.wait_ge(s_bdz, 1)
            gates(0)
            pool.wait_ge(s_pe, 2 * (PLE0 + 1))
            pool.memset(BD[:, :, :, :], 0.0).then_inc(s_bdz, 1)
            pool.memset(RIN[:, :, 0:3], 0.0).then_inc(s_bdz, 1)
            pool.wait_ge(s_bdz, 3)
            gates(1)
            pool.wait_ge(s_hf, 4 * 5)
            pool.memset(FACC[:, :, :], 0.0).then_inc(m_z, 1)
            pool.memset(Y[:, :], 0.0).then_inc(m_z, 1)
            pool.memset(S[:, :], 0.0).then_inc(m_z, 1)

        @block.scalar
        def _(act):
            chain = [0]

            def link(ins):
                chain[0] += 1
                ins.then_inc(s_ac, 1)
                act.wait_ge(s_ac, chain[0])

            for s, n in ((f_s, 2), (m_s, 2), (m_y0, 1)):
                act.sem_inc(s, n)

            def load(dst, src, s=s_ld):
                act.dma_start(dst, src).then_inc(s, 16)

            for blk in range(BLK):
                load(XT[:, blk, :], x[0, P * blk:P * blk + P, :], s_ldx)
            load(R1[0:96, :], norm_g.rearrange("l n (t p) -> (l n t) p", p=P))
            load(R1[96:98, :], subln_g)
            at_row = 0
            for v in (conv_w.rearrange("l j (t p) -> (l j t) p", p=P), conv_b.rearrange("l (t p) -> (l t) p", p=P),
                      lru_ba.rearrange("l (t p) -> (l t) p", p=P), lru_bx.rearrange("l (t p) -> (l t) p", p=P),
                      lru_lam.rearrange("l (t p) -> (l t) p", p=P)):
                n = v.shape[0]
                load(R2[at_row:at_row + n, :], v)
                at_row += n
            load(PT[:, :, :], p.rearrange("l b (k t) d -> t (l b k) d", t=P))
            load(POSI[:, :], positions.partition_broadcast(P)[:, 0, :])
            load(DL[:, :, :], diff_lambda.rearrange("l j d -> (l j) d").partition_broadcast(P))
            load(IFR[:, :], inv_freq)
            load(RW[:, :, :], rows(router_w[0]))

            def hi(b, jobs=0):
                act.wait_ge(s_w[b % RAW], 16 * (b // RAW + 1) + 16 * (FFN // RAW) * jobs)
                for e in range(2):
                    if not (isinstance(jobs, int) and b + FFN * jobs < SPL):
                        act.wait_ge(s_pe, 2 * (b - SPL) + e + 1 + 2 * FFN * jobs)
                    r = slice(HC * e, HC * e + HC)
                    nc.scalar.activation(whi[b % SPL][:, r], raw[b % RAW][:, r], ACT.Copy).then_inc(s_hi, 1)

            for n in range(4):
                act.wait_ge(s_tp, n + 1)
                nc.scalar.activation(XF[:, 2 * n:2 * n + 2, :], B[n][:, :].rearrange("p (t s) -> p t s", t=2),
                                     ACT.Copy).then_inc(s_xn, 1)

            for n in range(2):
                act.wait_ge(s_tp, 5 + n)
                nc.scalar.activation(PF[:, n, :, :], B[4 + n][:, :].rearrange("p (t s) -> p t s", t=2),
                                     ACT.Copy).then_inc(s_tc, 1)
            act.wait_ge(s_tp, 7)
            nc.scalar.activation(V1[:, :], B[6][:, 0:98], ACT.Copy).then_inc(s_tc, 1)
            nc.scalar.activation(V2[:, :], B[6][:, 128:256], ACT.Copy).then_inc(s_tc, 1)
            act.wait_ge(s_c0, 1)
            nc.scalar.activation(SM[:, 0:16], SM[:, 16:32], ACT.Exp).then_inc(s_c1, 1)
            nc.scalar.activation(SM[:, 64:68], SM[:, 68:72], ACT.Exp).then_inc(s_c1, 1)
            act.wait_ge(s_r0, 1)
            nc.scalar.activation(SIN[:, :], TT[:, 0, :], ACT.Sin).then_inc(s_r1, 1)
            nc.scalar.activation(COS[:, :], TT[:, 1, :], ACT.Sin).then_inc(s_r1, 1)
            for b in range(SPL):
                hi(b)

            def prenorm(m, split=True):
                for i in range(4):
                    act.wait_ge(s_xn, 4 * m + i + 1)
                    nc.scalar.activation(ZSQ[:, 2 * i:2 * i + 2, :], XF[:, 2 * i:2 * i + 2, :],
                                         ACT.Square).then_inc(s_xq, 1)
                act.wait_ge(s_xm, m + 1)
                nc.scalar.activation(STD[:, :], B[7][:, 0:SEQ], ACT.Sqrt, bias=EPSC[:, 0:1],
                                     scale=1.0 / D).then_inc(s_xs, 1)
                for i in range(4 if split else 0):
                    act.wait_ge(s_hf, 4 * m + i + 1)
                    nc.scalar.activation(HH[:, 2 * i:2 * i + 2, :], HF[:, 2 * i:2 * i + 2, :],
                                         ACT.Copy).then_inc(s_hh, 1)

            def postnorm(n):
                act.wait_ge(s_zm, n + 1)
                nc.scalar.activation(STD[:, :], B[3][:, 0:SEQ], ACT.Sqrt, bias=EPSC[:, 0:1],
                                     scale=1.0 / D).then_inc(s_zs, 1)

            def pair(t, i):
                return t[:, 2 * i:2 * i + 2, :]

            def bank2(n):
                return B[n][:, :].rearrange("p (t s) -> p t s", t=2)

            def gate_functions(layer, half):
                for i in range(4):
                    t = 4 * half + i
                    act.wait_ge(s_gt, KT * layer + t + 1)
                    if i == 0 and half == 1:
                        act.wait_ge(s_rh, 2 * layer + 1)
                    bank = B[3 if t % 2 == 0 else 7]
                    col = layer * KT + t
                    link(nc.scalar.activation(T2[:, i, :], bank[:, 0:SEQ], ACT.Sigmoid, bias=V2[:, 80 + col:81 + col]))
                    nc.scalar.activation(IG[:, i, :], bank[:, SEQ:], ACT.Sigmoid, bias=V2[:, 96 + col:97 + col])
                    ins = nc.scalar.activation(T2[:, i, :], T2[:, i, :], ACT.Tanh, scale=SPLAM[:, col:col + 1])
                    ins.then_inc(s_ga, 1)
                act.wait_ge(s_ga, KT * layer + 4 * half + 4)
                nc.scalar.activation(SQ[:, :, :], T2[:, :, :], ACT.Sqrt).then_inc(s_sq, 1)

            def mixer(layer):
                b = BASE[layer]
                for c in range(MIX):
                    hi(b + c + SPL)
                    if c < 4:
                        if c == 0 and layer == 1:
                            act.wait_ge(s_bdz, 3)
                        nc.scalar.activation(RIN[:, 2 * c:2 * c + 2, 3:], bank2(c % 3), ACT.Copy).then_inc(s_eva, 1)
                    elif c < 8:
                        nc.scalar.activation(pair(GEL, c - 4), bank2(c % 3), ACT.Gelu_apprx_tanh).then_inc(s_eva, 1)
                    elif c < 16:
                        i = c - 8
                        n = 8 * layer + i
                        if i >= 2:
                            act.wait_ge(s_qr, n - 1)
                        nc.scalar.activation(QT[:, i % 2, :, :], bank2(c % 3), ACT.Copy).then_inc(s_eva, 1)
                    elif c < 20:
                        nc.scalar.activation(V[:, :, 256 * (c - 16):256 * (c - 15)], bank2(c % 3),
                                             ACT.Copy).then_inc(s_eva, 1)
                    elif c < 24:
                        if c == 20:
                            act.wait_ge(s_qr, 8 * layer + 8)
                        nc.scalar.activation(pair(SGA, c - 20), bank2(c % 3), ACT.Tanh, scale=0.5).then_inc(s_eva, 1)
                    elif c < 28:
                        if c == 24:
                            act.wait_ge(s_ya, layer + 1)
                        nc.scalar.activation(pair(SGB, c - 24), bank2(c % 3), ACT.Tanh, scale=0.5).then_inc(s_eva, 1)
                    elif c >= 36:
                        i = c - 36
                        nc.scalar.activation(pair(Z, i), bank2(c % 3), ACT.Copy)
                        nc.scalar.activation(pair(ZSQ, i), bank2(c % 3), ACT.Square).then_inc(s_eva, 1)
                    if c == 3:
                        gate_functions(layer, 0)
                    if c == 10:
                        gate_functions(layer, 1)
                    if c == 14:
                        act.wait_ge(s_rh, 2 * layer + 2)
                        nc.scalar.activation(YAH[:, :, :], GEL[:, :, :], ACT.Copy).then_inc(s_yh, 1)
                    h = c - 18
                    if 0 <= h < HEADS:
                        n = HEADS * layer + h
                        act.wait_ge(s_mx, n + 1)
                        sc, q = SC[:, h % 2, :], h % 2
                        for m in range(2):
                            nc.scalar.activation(sc[:, P * m:P * m + P], sc[:, P * m:P * m + P], ACT.Exp,
                                                 bias=AMX[:, q, m:m + 1], scale=HD ** -0.5,
                                                 accum_out=ASUM[:, q, m:m + 1])
                        for m in range(2):
                            r = sc[:, SEQ * (m + 1):SEQ * (m + 2)]
                            ins = nc.scalar.activation(r, r, ACT.Exp, bias=AMX[:, q, 2 + m:3 + m], scale=HD ** -0.5,
                                                       accum_out=ASUM[:, q, 2 + m:3 + m])
                        ins.then_inc(s_ex, 1)
                    h = c - 20
                    if 0 <= h < HEADS:
                        n = HEADS * layer + h
                        act.wait_ge(s_wt, n + 1)
                        if h >= 2:
                            act.wait_ge(s_o, n - 1)
                        nc.scalar.activation(WT[:, h % 2, :], B[6][:, 0:384], ACT.Copy).then_inc(s_wc, 1)
                    h = c - 21
                    if 0 <= h < HEADS:
                        n = HEADS * layer + h
                        act.wait_ge(s_o, n + 1)
                        if h >= 2:
                            act.wait_ge(s_om, n - 1)
                        nc.scalar.activation(OALL[:, h, :], B[7][:, 0:SEQ], ACT.Copy)
                        nc.scalar.activation(OSQ[:, h % 2, :], B[7][:, 0:SEQ], ACT.Square).then_inc(s_oc, 1)
                    h = c - 22
                    if 0 <= h < HEADS:
                        n = HEADS * layer + h
                        act.wait_ge(s_om, n + 1)
                        nc.scalar.activation(MSALL[:, h, :], B[3][:, 0:SEQ], ACT.Copy).then_inc(s_oe, 1)
                    if c == 30:
                        act.wait_ge(s_oe, HEADS * (layer + 1))
                        for g in range(2):
                            r = MSALL[:, 4 * g:4 * g + 4, :]
                            nc.scalar.activation(r, r, ACT.Sqrt, bias=EPSC[:, 0:1], scale=1.0 / P).then_inc(s_os, 1)
                        for g in range(2):
                            act.wait_ge(s_yf, 2 * layer + g + 1)
                            nc.scalar.activation(YBH[:, 4 * g:4 * g + 4, :], OALL[:, 4 * g:4 * g + 4, :],
                                                 ACT.Copy).then_inc(s_ybh, 1)
                    if 32 <= c < 36:
                        i = c - 32
                        act.wait_ge(s_m, 4 * layer + i + 1)
                        nc.scalar.activation(pair(YAH, i), pair(SGB, i), ACT.Copy, scale=0.5).then_inc(s_mh, 1)

            def split_p(layer):
                nc.scalar.activation(PHI[:, :, :], PF[:, layer, :, :], ACT.Copy).then_inc(s_ph, 1)

            def embed(b, jobs, layer):
                hi(b + SPL, jobs)
                for n in range(4):
                    ins = nc.scalar.activation(pair(PP, n), bank2(n), ACT.Copy)
                ins.then_inc(s_pp, 1)

            def embed_gates(b, jobs, z0, last):
                for i in range(4):
                    if i < 1 or not last:
                        hi(b + 1 + i + SPL, jobs)
                    else:
                        act.wait_ge(s_pe, 2 * (b + 2 + i) + 2 * FFN * jobs)
                    if i >= 2:
                        act.wait_ge(s_zp, z0 + i - 1)
                    nc.scalar.activation(PG[:, i % 2, :], B[4 + i][:, :], ACT.Sigmoid).then_inc(s_pg, 1)
                    if i >= 1:
                        square_z(z0 + i, i - 1, Z)
                square_z(z0 + 4, 3, Z)

            def square_z(n, i, z):
                act.wait_ge(s_zp, n)
                nc.scalar.activation(pair(ZSQ, i), pair(z, i), ACT.Square).then_inc(s_zq, 1)

            prenorm(0)
            mixer(0)
            postnorm(0)
            prenorm(1)

            def dense(s, it, q):
                b = FFN0 + 2 * q
                for n in range(2):
                    nb = b + n + SPL
                    act.wait_ge(s_w[nb % RAW], 16 * (nb // RAW + 1) + 32 * it)
                    for e in range(2):
                        act.wait_ge(s_pe, 2 * (b + n) + e + 1 + 24 * it)
                        r = slice(HC * e, HC * e + HC)
                        nc.scalar.activation(whi[nb % SPL][:, r], raw[nb % RAW][:, r], ACT.Copy).then_inc(s_hi, 1)
                    if n == 0:
                        act.wait_ge(f_a, s + 1)
                        nc.scalar.activation(FS[:, q % 2, :], B[2 * (q % 2)][:, :], ACT.Silu).then_inc(f_s, 1)
                act.wait_ge(f_a, s + 3)
                nc.scalar.activation(FH[:, bass.ds(2 * s, 2), :] if not isinstance(s, int) else pair(FH, s),
                                     FA[:, q % 2, :].rearrange("p (t s) -> p t s", t=2), ACT.Copy).then_inc(f_h, 1)

            with act.Fori(0, 2) as it:
                for q in range(6):
                    dense(6 * it + q, it, q)
            for q in range(2):
                dense(12 + q, 2, q)
            for d in range(14):
                hi(FFN0 + GU + d + SPL)
            for i in range(4):
                square_z(i + 1, i, Z)
            split_p(0)
            postnorm(1)
            embed(PLE0, 0, 0)
            prenorm(2)
            embed_gates(PLE0, 0, 4, False)
            postnorm(2)
            prenorm(3)
            mixer(1)
            postnorm(3)
            prenorm(4, split=False)

            act.wait_ge(r_d, 1)
            nc.scalar.activation(SM[:, 52:54], SM[:, 50:52], ACT.Exp).then_inc(r_e, 1)
            for n in range(4):
                act.wait_ge(r_tp, n + 1)
                nc.scalar.activation(HTH[:, n // 2, 512 * (n % 2):512 * (n % 2) + 512], B[2 + n][:, :],
                                     ACT.Copy).then_inc(r_th, 1)
            for u in range(2):
                act.wait_ge(m_p7, u + 1)
                nc.scalar.activation(XGH[:, 4 * u:4 * u + 4, :], B[7][:, :].rearrange("p (t s) -> p t s", t=4),
                                     ACT.Copy).then_inc(m_b7, 1)
            act.wait_ge(r_j, 1)
            jobs = act.value_load(JINFO[0:1, 0:1], min_val=EXPERTS, max_val=MAX_JOBS)
            with act.Fori(0, jobs) as j:
                for c in range(FFN):
                    hi(MOE0 + c + SPL, j)
                    if c < GU and c % 4 == 1:
                        f = c // 4
                        act.wait_ge(m_a, 7 * j + (f + 1 if f else 2))
                        nc.scalar.activation(MS[:, f % 2, :], B[2 * (f % 2)][:, :], ACT.Silu).then_inc(m_s, 1)
                    if c % 4 == 2 and 6 <= c <= 30:
                        f = (c - 6) // 4
                        act.wait_ge(m_t, 7 * j + f + 1)
                        nc.scalar.activation(ATH[:, 4 * f:4 * f + 4, :], B[6][:, :].rearrange("p (t s) -> p t s", t=4),
                                             ACT.Copy).then_inc(m_th, 1)
                    if c in GATHER[:2]:
                        u = GATHER.index(c)
                        act.wait_ge(m_p7, 4 + U7 * j + 5 + u + 1)
                        nc.scalar.activation(XGH[:, 4 * u:4 * u + 4, :],
                                             B[7][:, :].rearrange("p (t s) -> p t s", t=4), ACT.Copy).then_inc(m_b7, 1)
                nc.scalar.activation(Y[:, 0:512], B[4][:, :], ACT.Copy).then_inc(m_y0, 1)
            for i in range(4):
                square_z(8 + i + 1, i, FACC)
            split_p(1)
            postnorm(4)
            embed(MOE0, jobs, 1)
            prenorm(5)
            embed_gates(MOE0, jobs, 12, True)
            postnorm(5)
            for n in range(4):
                act.wait_ge(s_ot, n + 1)
                nc.scalar.activation(OT[:, n // 2, 512 * (n % 2):512 * (n % 2) + 512], B[n][:, :],
                                     ACT.Copy).then_inc(s_oo, 1)


        @block.vector
        def _(dve):
            chain = [0]

            def mark(ins):
                chain[0] += 1
                ins.then_inc(s_dc, 1)
                return chain[0]

            def link(ins):
                dve.wait_ge(s_dc, mark(ins))

            v = nc.vector

            def pair(t, i):
                return t[:, 2 * i:2 * i + 2, :]

            def bank2(n):
                return B[n][:, :].rearrange("p (t s) -> p t s", t=2)

            def lo(b, jobs=0):
                for e in range(2):
                    dve.wait_ge(s_hi, 2 * b + e + 1 + 2 * FFN * jobs)
                    r = slice(HC * e, HC * e + HC)
                    v.tensor_tensor(wlo[b % SPL][:, r], raw[b % RAW][:, r], whi[b % SPL][:, r].bitcast(F32),
                                    ALU.subtract).then_inc(s_lo, 1)

            for s, n in ((f_a, 2), (m_a, 2), (m_tl, 1), (m_y1, 1)):
                dve.sem_inc(s, n)

            dve.wait_ge(s_ld, 16 * N_LD)
            link(v.tensor_copy(POSF[:, :], POSI[:, :]))
            link(v.tensor_scalar(TT[:, 0, :], POSF[:, :], IFR[:, 0:1], None, ALU.mult))
            magic = 1.5 * 2.0 ** 23
            link(v.tensor_scalar(TT[:, 1, :], TT[:, 0, :], 1.0 / (2 * math.pi), None, ALU.mult))
            link(v.tensor_scalar(TT[:, 1, :], TT[:, 1, :], magic, None, ALU.add))
            link(v.tensor_scalar(TT[:, 1, :], TT[:, 1, :], -magic, None, ALU.add))
            c1 = 6.28125
            c2 = math.floor((2 * math.pi - c1) * 2.0 ** 20) / 2.0 ** 20
            c3 = 2 * math.pi - c1 - c2
            for c in (c1, c2, c3):
                link(v.scalar_tensor_tensor(out=TT[:, 0, :], in0=TT[:, 1, :], scalar=-c, in1=TT[:, 0, :],
                                            op0=ALU.mult, op1=ALU.add))
            link(v.tensor_scalar(TT[:, 0, :], TT[:, 0, :], 3.1415925, -3.1415925, ALU.min, ALU.max))
            link(v.scalar_tensor_tensor(out=TT[:, 2, :], in0=TT[:, 0, :], scalar=-1.0, in1=TT[:, 0, :],
                                        op0=ALU.mult, op1=ALU.max))
            v.tensor_scalar(TT[:, 1, :], TT[:, 2, :], -1.0, math.pi / 2, ALU.mult, ALU.add).then_inc(s_r0, 1)

            dve.wait_ge(s_tc, 4)
            lam = V2[:, 112:128]
            v.scalar_tensor_tensor(out=SM[:, 16:32], in0=lam, scalar=-1.0, in1=lam, op0=ALU.mult, op1=ALU.min)
            v.tensor_scalar(SM[:, 32:48], lam, -1.0, 0.0, ALU.mult, ALU.max)
            dl = DL[:, :, :].rearrange("p (a b) d -> p a b d", b=2)
            link(v.tensor_tensor(TT[:, 3, :].rearrange("p (a d) -> p a d", a=4), dl[:, :, 0, :], dl[:, :, 1, :],
                                 ALU.mult))
            v.tensor_reduce(SM[:, 68:72], TT[:, 3, :].rearrange("p (a d) -> p a d", a=4), AX.X,
                            ALU.add).then_inc(s_c0, 1)
            dve.wait_ge(s_c1, 2)
            for layer in range(DEPTH):
                init = 0.8 - 0.6 * math.exp(-0.3 * layer)
                link(v.tensor_tensor(NLAM[:, layer:layer + 1], SM[:, 65 + 2 * layer:66 + 2 * layer],
                                     SM[:, 64 + 2 * layer:65 + 2 * layer], ALU.subtract))
                v.tensor_scalar(NLAM[:, layer:layer + 1], NLAM[:, layer:layer + 1], -init, None, ALU.add)
                v.tensor_scalar(GSUB[:, layer:layer + 1], V1[:, 96 + layer:97 + layer], 1.0 - init, None, ALU.mult)
            y, s1, s2, poly = SM[:, 0:16], SM[:, 72:88], SM[:, 88:104], SM[:, 104:120]
            link(v.tensor_scalar(s1, y, 2.0, None, ALU.add))
            link(v.reciprocal(s1, s1))
            link(v.tensor_tensor(s1, s1, y, ALU.mult))
            link(v.tensor_tensor(s2, s1, s1, ALU.mult))
            link(v.tensor_scalar(poly, s2, 1.0 / 17, None, ALU.mult))
            for n in (15, 13, 11, 9, 7, 5, 3):
                link(v.scalar_tensor_tensor(out=poly, in0=poly, scalar=1.0 / n, in1=s2, op0=ALU.add, op1=ALU.mult))
            link(v.scalar_tensor_tensor(out=poly, in0=poly, scalar=1.0, in1=s1, op0=ALU.add, op1=ALU.mult))
            link(v.scalar_tensor_tensor(out=poly, in0=poly, scalar=2.0, in1=SM[:, 32:48], op0=ALU.mult, op1=ALU.add))
            link(v.tensor_scalar(SPLAM[:, :], poly, 4.0, None, ALU.mult))
            for b in range(SPL):
                lo(b)

            def gcol(layer, n, t):
                i = (layer * N_NORMS + n) * KT + t
                return V1[:, i:i + 1]

            def prenorm(m, split=True):
                layer, n = m // 3, 2 * (m % 3)
                dve.wait_ge(s_xs, m + 1)
                link(v.reciprocal(RINV[:, :], STD[:, :]))

                def normal(i):
                    for t in (2 * i, 2 * i + 1):
                        ins = v.scalar_tensor_tensor(out=HF[:, t, :], in0=XF[:, t, :], scalar=gcol(layer, n, t),
                                                     in1=RINV[:, :], op0=ALU.mult, op1=ALU.mult)
                    ins.then_inc(s_hf, 1)

                def rest(i):
                    dve.wait_ge(s_hh, 4 * (m if m < 4 else m - 1) + i + 1)
                    v.tensor_tensor(pair(HL, i), pair(HF, i), pair(HH, i).bitcast(F32), ALU.subtract).then_inc(s_hl, 1)

                normal(0)
                for i in range(1, 4):
                    normal(i)
                    if split:
                        rest(i - 1)
                if split:
                    rest(3)

            def postnorm(n, z):
                layer, g = n // 3, 2 * (n % 3) + 1
                dve.wait_ge(s_zs, n + 1)
                link(v.reciprocal(RINV[:, :], STD[:, :]))
                done = []

                def normal(i):
                    for t in (2 * i, 2 * i + 1):
                        ins = v.scalar_tensor_tensor(out=z[:, t, :], in0=z[:, t, :], scalar=gcol(layer, g, t),
                                                     in1=RINV[:, :], op0=ALU.mult, op1=ALU.mult)
                    done.append(mark(ins))

                def add(i):
                    dve.wait_ge(s_dc, done[i])
                    v.tensor_tensor(pair(XF, i), pair(XF, i), pair(z, i), ALU.add).then_inc(s_xn, 1)

                normal(0)
                for i in range(1, 4):
                    normal(i)
                    add(i - 1)
                add(3)

            def convolve(layer, j):
                dve.wait_ge(s_eva, eva(layer, j))
                if j == 2:
                    dve.wait_ge(s_gt, KT * layer + 4)
                for tap in range(4):
                    for i in range(2):
                        t = 2 * j + i
                        w = V2[:, (layer * 4 + tap) * KT + t:(layer * 4 + tap) * KT + t + 1]
                        u = U[:, t % 4, :]
                        r = RIN[:, t, tap:tap + SEQ]
                        if tap == 0:
                            col = 64 + layer * KT + t
                            ins = v.tensor_scalar(u, r, w, V2[:, col:col + 1], ALU.mult, ALU.add)
                        else:
                            ins = v.scalar_tensor_tensor(out=u, in0=r, scalar=w, in1=u, op0=ALU.mult, op1=ALU.add)
                    if tap < 3:
                        link(ins)
                    else:
                        ins.then_inc(s_u, 1)

            def recurrence(layer, half):
                dve.wait_ge(s_sq, 2 * layer + half + 1)
                f = lambda t: t[:, :, :]
                link(v.tensor_scalar(f(T2), f(T2), 1.0, None, ALU.add))
                v.tensor_tensor(f(IG), f(IG), f(U), ALU.mult)
                link(v.reciprocal(f(T2), f(T2)))
                link(v.scalar_tensor_tensor(out=f(SQ), in0=f(SQ), scalar=2.0, in1=f(T2), op0=ALU.mult, op1=ALU.mult))
                v.tensor_scalar(f(T2), f(T2), 2.0, -1.0, ALU.mult, ALU.add)
                return mark(v.tensor_tensor(f(IG), f(IG), f(SQ), ALU.mult))

            def scans(after):
                dve.wait_ge(s_dc, after)
                for i in range(4):
                    ins = v.tensor_tensor_scan(IG[:, i, :], T2[:, i, :], IG[:, i, :], 0.0, ALU.mult, ALU.add)
                return mark(ins)

            def gate_y(layer, half, after):
                dve.wait_ge(s_dc, after)
                dve.wait_ge(s_eva, eva(layer, 4 + 2 * half + 1))
                g = GEL[:, 4 * half:4 * half + 4, :]
                v.tensor_tensor(g, IG[:, :, :], g, ALU.mult).then_inc(s_rh, 1)

            def rotate(layer, i):
                n = 8 * layer + i
                dst = pair(Q, i) if i < 4 else pair(K, i - 4)
                cos, sin = (t[:, :].unsqueeze(1).to_broadcast([P, 2, SEQ]) for t in (COS, SIN))
                if n == 0:
                    dve.wait_ge(s_r1, 2)
                dve.wait_ge(s_qs, n + 1)
                v.tensor_tensor(QS[:, :, :], bank2(6), sin, ALU.mult)
                link(v.tensor_tensor(dst, QT[:, i % 2, :, :], cos, ALU.mult))
                v.tensor_tensor(dst, dst, QS[:, :, :], ALU.add).then_inc(s_qr, 1)

            def mask_max(layer, h):
                n, q = HEADS * layer + h, h % 2
                dve.wait_ge(s_sc, n + 1)
                if h >= 2:
                    dve.wait_ge(s_wt, n - 1)
                for m in range(2):
                    v.tensor_tensor_reduce(SC[:, q, P * m:P * m + P], B[4 + m][:, 0:P], MASK[:, P:SEQ], 1.0,
                                           -3e38, ALU.add, ALU.max, AMX[:, q, m:m + 1])
                for m in range(2):
                    ins = v.tensor_tensor_reduce(SC[:, q, SEQ * (m + 1):SEQ * (m + 2)], B[4 + m][:, P:P + SEQ],
                                                 MASK[:, :], 1.0, -3e38, ALU.add, ALU.max, AMX[:, q, 2 + m:3 + m])
                link(ins)
                v.tensor_scalar(AMX[:, q, :], AMX[:, q, :], -HD ** -0.5, None, ALU.mult).then_inc(s_mx, 1)

            def difference(layer, h):
                n, q = HEADS * layer + h, h % 2
                dve.wait_ge(s_ex, n + 1)
                link(v.reciprocal(AR[:, q, :], ASUM[:, q, :]))
                odd = AR[:, q, :].rearrange("p (b m) -> p b m", m=2)[:, :, 1]
                v.tensor_scalar(odd, odd, NLAM[:, layer:layer + 1], None, ALU.mult)
                for b, r in ((0, SC[:, q, 0:P]), (1, SC[:, q, SEQ:2 * SEQ])):
                    ins = v.tensor_scalar(r, r, AR[:, q, 2 * b:2 * b + 1], None, ALU.mult)
                link(ins)
                v.scalar_tensor_tensor(out=SC[:, q, 0:P], in0=SC[:, q, P:2 * P], scalar=AR[:, q, 1:2],
                                       in1=SC[:, q, 0:P], op0=ALU.mult, op1=ALU.add)
                v.scalar_tensor_tensor(out=SC[:, q, SEQ:2 * SEQ], in0=SC[:, q, 2 * SEQ:3 * SEQ],
                                       scalar=AR[:, q, 3:4], in1=SC[:, q, SEQ:2 * SEQ], op0=ALU.mult,
                                       op1=ALU.add).then_inc(s_df, 1)

            def normalise_heads(layer):
                for g in range(2):
                    ms, o = (t[:, 4 * g:4 * g + 4, :] for t in (MSALL, OALL))
                    dve.wait_ge(s_os, 2 * layer + g + 1)
                    link(v.reciprocal(ms, ms))
                    v.scalar_tensor_tensor(out=o, in0=o, scalar=GSUB[:, layer:layer + 1], in1=ms, op0=ALU.mult,
                                           op1=ALU.mult).then_inc(s_yf, 1)
                for g in range(2):
                    dve.wait_ge(s_ybh, 2 * layer + g + 1)
                    r = lambda t: t[:, 4 * g:4 * g + 4, :]
                    v.tensor_tensor(r(YBL), r(OALL), r(YBH).bitcast(F32), ALU.subtract).then_inc(s_yb, 1)

            def mixer(layer):
                b = BASE[layer]
                after = 0
                for c in range(MIX):
                    lo(b + c + SPL)
                    if c in (0, 1, 6, 7):
                        convolve(layer, c if c < 2 else c - 4)
                    if c in (4, 12):
                        after = recurrence(layer, c // 12)
                    if c in (5, 13):
                        after = scans(after)
                    if c in (8, 14):
                        gate_y(layer, c // 14, after)
                    if 9 <= c < 17:
                        rotate(layer, c - 9)
                    if c == 15:
                        dve.wait_ge(s_yh, layer + 1)
                        v.tensor_tensor(YAL[:, :, :], GEL[:, :, :], YAH[:, :, :].bitcast(F32),
                                        ALU.subtract).then_inc(s_ya, 1)
                    if 18 <= c < 26:
                        mask_max(layer, c - 18)
                    if 19 <= c < 27:
                        difference(layer, c - 19)
                    if 28 <= c < 32:
                        i = c - 28
                        v.scalar_tensor_tensor(out=pair(SGA, i), in0=pair(SGA, i), scalar=1.0, in1=bank2(c % 3),
                                               op0=ALU.add, op1=ALU.mult).then_inc(s_evd, 1)
                    if c == 30:
                        normalise_heads(layer)
                    if 32 <= c < 36:
                        i = c - 32
                        v.scalar_tensor_tensor(out=pair(SGB, i), in0=pair(SGB, i), scalar=1.0, in1=bank2(c % 3),
                                               op0=ALU.add, op1=ALU.mult).then_inc(s_evd, 1)
                        dve.wait_ge(s_evd, evd(layer, c))
                        v.tensor_tensor(pair(SGB, i), pair(SGB, i), pair(SGA, i), ALU.add).then_inc(s_m, 1)
                        dve.wait_ge(s_mh, 4 * layer + i + 1)
                        v.scalar_tensor_tensor(out=pair(YAL, i), in0=pair(SGB, i), scalar=0.5,
                                               in1=pair(YAH, i).bitcast(F32), op0=ALU.mult,
                                               op1=ALU.subtract).then_inc(s_ml, 1)

            def split_p(layer):
                dve.wait_ge(s_ph, layer + 1)
                v.tensor_tensor(PLO[:, :, :], PF[:, layer, :, :], PHI[:, :, :].bitcast(F32),
                                ALU.subtract).then_inc(s_pl, 1)

            def embed_gates(b, jobs, layer, last):
                for i in range(4):
                    if i < 1 or not last:
                        lo(b + 1 + i + SPL, jobs)
                    if i == 0:
                        dve.wait_ge(s_pp, layer + 1)
                    dve.wait_ge(s_pg, 4 * layer + i + 1)
                    v.tensor_tensor(pair(Z, i), PG[:, i % 2, :].rearrange("p (t s) -> p t s", t=2), pair(PP, i),
                                    ALU.mult).then_inc(s_zp, 1)

            prenorm(0)
            mixer(0)
            postnorm(0, Z)
            prenorm(1)

            def dense(s, it, q):
                b = FFN0 + 2 * q
                for n in range(2):
                    nb = b + n + SPL
                    for e in range(2):
                        dve.wait_ge(s_hi, 2 * nb + e + 1 + 24 * it)
                        r = slice(HC * e, HC * e + HC)
                        v.tensor_tensor(wlo[nb % SPL][:, r], raw[nb % RAW][:, r], whi[nb % SPL][:, r].bitcast(F32),
                                        ALU.subtract).then_inc(s_lo, 1)
                dve.wait_ge(f_s, s + 3)
                v.tensor_tensor(FA[:, q % 2, :], FS[:, q % 2, :], B[2 * (q % 2) + 1][:, :], ALU.mult).then_inc(f_a, 1)
                dve.wait_ge(f_h, s + 1)
                at_s = (slice(None), bass.ds(2 * s, 2) if not isinstance(s, int) else slice(2 * s, 2 * s + 2))
                v.tensor_tensor(FL[at_s[0], at_s[1], :], FA[:, q % 2, :].rearrange("p (t s) -> p t s", t=2),
                                FH[at_s[0], at_s[1], :].bitcast(F32), ALU.subtract).then_inc(f_l, 1)

            with dve.Fori(0, 2) as it:
                for q in range(6):
                    dense(6 * it + q, it, q)
            for q in range(2):
                dense(12 + q, 2, q)
            for d in range(14):
                lo(FFN0 + GU + d + SPL)
            for i in range(4):
                v.tensor_copy(pair(Z, i), bank2(4 + i)).then_inc(s_zp, 1)
            dve.wait_ge(s_zp, 4)
            split_p(0)
            postnorm(1, Z)
            lo(PLE0 + SPL)
            prenorm(2)
            embed_gates(PLE0, 0, 0, False)
            postnorm(2, Z)
            prenorm(3)
            mixer(1)
            postnorm(3, Z)
            prenorm(4, split=False)

            def rt(n):
                return RT[:, n, :, :]

            def rt1(n):
                return RT[:, n, :, 0:1]

            def wide(n):
                return RT[:, n, :, 0:1].to_broadcast([P, BLK, EXPERTS])

            desc = SM[:, 120:136].rearrange("p (b e) -> p b e", b=BLK)
            for b in range(BLK):
                v.tensor_scalar(desc[:, b, :], IOTA[:, 0:EXPERTS], -1.0, float(EXPERTS), ALU.mult, ALU.add)
            LG, KEY, O1, O2, M1, M2, K1, W1, W2, SEL, COMB, RK, CNT, TMP = range(14)
            dve.wait_ge(r_lg, 1)
            link(v.tensor_copy(rt(LG), B[0][:, 0:2 * EXPERTS].rearrange("p (b e) -> p b e", b=BLK)))
            for one, top in ((O1, M1), (O2, M2)):
                link(v.tensor_reduce(rt1(top), rt(LG), AX.X, ALU.max))
                link(v.tensor_tensor(rt(KEY), rt(LG), wide(top), ALU.is_equal))
                link(v.tensor_tensor(rt(KEY), rt(KEY), desc, ALU.mult))
                link(v.tensor_reduce(rt1(K1), rt(KEY), AX.X, ALU.max))
                link(v.tensor_tensor(rt(one), rt(KEY), wide(K1), ALU.is_equal))
                link(v.scalar_tensor_tensor(out=rt(LG), in0=rt(one), scalar=-3e38, in1=rt(LG), op0=ALU.mult,
                                            op1=ALU.add))
            v.tensor_tensor(SM[:, 50:52].rearrange("p (b e) -> p b e", b=BLK), rt1(M2), rt1(M1),
                            ALU.subtract).then_inc(r_d, 1)
            v.tensor_tensor(rt(SEL), rt(O1), rt(O2), ALU.add).then_inc(r_sel, 1)
            dve.wait_ge(r_e, 1)
            ex = SM[:, 52:54].rearrange("p (b e) -> p b e", b=BLK)
            link(v.tensor_scalar(rt1(W1), ex, 1.0, None, ALU.add))
            link(v.reciprocal(rt1(W1), rt1(W1)))
            link(v.tensor_tensor(rt1(W2), rt1(W1), ex, ALU.mult))
            v.tensor_tensor(rt(COMB), rt(O1), wide(W1), ALU.mult)
            link(v.tensor_tensor(rt(TMP), rt(O2), wide(W2), ALU.mult))
            link(v.tensor_tensor(rt(COMB), rt(COMB), rt(TMP), ALU.add))
            v.tensor_copy(JC[:, :, 0:EXPERTS], rt(COMB))
            for n in range(4):
                dve.wait_ge(r_th, n + 1)
                r = (slice(None), n // 2, slice(512 * (n % 2), 512 * (n % 2) + 512))
                v.tensor_tensor(HTL[r[0], r[1], r[2]], B[2 + n][:, :], HTH[r[0], r[1], r[2]].bitcast(F32),
                                ALU.subtract).then_inc(r_tl, 1)
            dve.wait_ge(r_rk, 1)
            link(v.scalar_tensor_tensor(out=rt(RK), in0=B[1][:, 0:16].rearrange("p (b e) -> p b e", b=BLK),
                                        scalar=1.0, in1=rt(SEL), op0=ALU.add, op1=ALU.mult))
            link(v.tensor_scalar(JR[:, :, 0:EXPERTS], rt(RK), -1.0, None, ALU.add))

            def selection(col, sem_):
                for b in range(BLK):
                    ins = v.tensor_scalar(DSEL[:, b, :], IOTA[:, :], JR[:, b, col], None, ALU.is_equal)
                ins.then_inc(sem_, 1)

            selection(slice(0, 1), m_d)
            over, count = RT[:, CNT, 0, :], RT[:, CNT, 1, :]
            link(v.tensor_scalar(over, B[1][:, 16:24], float(TOKENS), None, ALU.is_gt))
            link(v.memset(RT[:, TMP, 0, :], 0.0))
            link(v.tensor_tensor_scan(count, over, RT[:, TMP, 0, :], 0.0, ALU.add, ALU.add))
            link(v.tensor_scalar(SM[:, 140:141], count[:, EXPERTS - 1:EXPERTS], float(EXPERTS), None, ALU.add))
            for e in range(MAX_EXTRA):
                mt, junk = RT[:, TMP, 0, :], RT[:, TMP, 1, :]
                link(v.tensor_scalar(mt, count, e + 1.0, None, ALU.is_equal))
                link(v.tensor_tensor(mt, mt, over, ALU.mult))
                link(v.tensor_tensor_reduce(junk, mt, IOTA[:, 0:EXPERTS], 1.0, 0.0, ALU.mult, ALU.add,
                                            SM[:, 141 + e:142 + e]))
                for b in range(BLK):
                    link(v.tensor_scalar(RT[:, W1, b, :], JR[:, b, 0:EXPERTS], -float(TOKENS), None, ALU.add))
                    link(v.tensor_tensor_reduce(junk, mt, RT[:, W1, b, :], 1.0, 0.0, ALU.mult, ALU.add,
                                                JR[:, b, EXPERTS + e:EXPERTS + e + 1]))
                    link(v.tensor_tensor_reduce(junk, mt, RT[:, COMB, b, :], 1.0, 0.0, ALU.mult, ALU.add,
                                                JC[:, b, EXPERTS + e:EXPERTS + e + 1]))
            v.tensor_copy(JINFO[:, :], SM[:, 140:144]).then_inc(r_j, 1)
            for u in range(2):
                dve.wait_ge(m_p7, 2 + u + 1)
                v.tensor_copy(XGL[:, 4 * u:4 * u + 4, :],
                              B[7][:, :].rearrange("p (t s) -> p t s", t=4)).then_inc(m_b7, 1)

            dve.wait_ge(r_j, 1)
            jobs = dve.value_load(JINFO[0:1, 0:1], min_val=EXPERTS, max_val=MAX_JOBS)
            with dve.Fori(0, jobs) as j:
                for c in range(FFN):
                    lo(MOE0 + c + SPL, j)
                    if c < GU and c % 4 == 3:
                        f = c // 4
                        dve.wait_ge(m_s, 7 * j + f + 3)
                        v.tensor_tensor(MA[:, f % 2, :], MS[:, f % 2, :], B[2 * (f % 2) + 1][:, :],
                                        ALU.mult).then_inc(m_a, 1)
                    if c in SCATTER:
                        i = SCATTER.index(c)
                        if i == 0:
                            dve.wait_ge(m_z, 3)
                        dve.wait_ge(m_p7, 4 + U7 * j + i + 1)
                        v.tensor_tensor(pair(FACC, i), pair(FACC, i), bank2(7), ALU.add).then_inc(m_b7, 1)
                    if c % 4 == 2 and 6 <= c <= 30:
                        f = (c - 6) // 4
                        dve.wait_ge(m_th, 7 * j + f + 1)
                        v.tensor_tensor(ATL[:, 4 * f:4 * f + 4, :], B[6][:, :].rearrange("p (t s) -> p t s", t=4),
                                        ATH[:, 4 * f:4 * f + 4, :].bitcast(F32), ALU.subtract).then_inc(m_tl, 1)
                    if c == TURN_W - 3:
                        for b in range(BLK):
                            ins = v.tensor_scalar(DC[:, b, :], IOTA[:, :], JR[:, b, bass.ds(j, 1)],
                                                  JC[:, b, bass.ds(j, 1)], ALU.is_equal, ALU.mult)
                        ins.then_inc(m_dc, 1)
                    if c == TURN_W:
                        dve.wait_ge(m_p7, 4 + U7 * j + 5)
                        v.tensor_copy(S[:, :], B[7][:, 0:SEQ]).then_inc(m_b7, 1)
                    if c == 20:
                        selection(bass.ds(j + 1, 1), m_d)
                    if c in GATHER[2:]:
                        u = GATHER.index(c) - 2
                        dve.wait_ge(m_p7, 4 + U7 * j + 7 + u + 1)
                        v.tensor_copy(XGL[:, 4 * u:4 * u + 4, :],
                                      B[7][:, :].rearrange("p (t s) -> p t s", t=4)).then_inc(m_b7, 1)
                v.tensor_copy(Y[:, 512:1024], B[5][:, :]).then_inc(m_y1, 1)
            for i in range(4):
                dve.wait_ge(m_p7, 4 + U7 * jobs + i + 1)
                v.tensor_tensor(pair(FACC, i), pair(FACC, i), bank2(7), ALU.add).then_inc(m_b7, 1)
                dve.wait_ge(m_b7, 4 + U7 * jobs + i + 1)
                dve.sem_inc(s_zp, 1)
            split_p(1)
            postnorm(4, FACC)
            lo(MOE0 + SPL, jobs)
            prenorm(5)
            embed_gates(MOE0, jobs, 1, True)
            postnorm(5, Z)

        @block.tensor
        def _(pe):
            mm = nc.tensor.matmul

            def three(dst, w, x, sl_w, sl_x, weights_stay, start, stop):
                wh, wl = w[0][sl_w], w[1][sl_w]
                xh, xl = x[0][sl_x], x[1][sl_x]
                terms = ((wh, xh), (wh, xl), (wl, xh)) if weights_stay else ((xh, wh), (xh, wl), (xl, wh))
                for n, (a, b) in enumerate(terms):
                    ins = mm(dst, a, b, start=start and n == 0, stop=stop and n == 2, skip_group_check=True)
                return ins

            A = slice(None)

            def wslot(b):
                return whi[b % SPL], wlo[b % SPL]

            def split(b, e, jobs=0, turns=0):
                pe.wait_ge(s_lo, 2 * b + e + 1 + 2 * FFN * jobs + 24 * turns)


            def chunk8(b, x, bank, ready=None, jobs=0, turns=0):
                for k in range(KT):
                    if k % 4 == 0:
                        split(b, k // 4, jobs, turns)
                    if ready:
                        ready(k)
                    for t in range(2):
                        ins = three(B[bank][:, SEQ * t:SEQ * t + SEQ], wslot(b), x,
                                    (A, slice(256 * k + P * t, 256 * k + P * t + P)), (A, k, A), True,
                                    k == 0 and t == 0, k == KT - 1)
                    if k % 4 == 3:
                        ins.then_inc(s_pe, 1)

            def chunk8v(b, x, bank):
                for k in range(KT):
                    if k % 4 == 0:
                        split(b, k // 4)
                    for t in range(BLK):
                        ins = three(B[bank][:, 256 * t:256 * t + 256], wslot(b), x,
                                    (A, slice(256 * k, 256 * k + 256)), (A, k, slice(P * t, P * t + P)), False,
                                    k == 0 and t == 0, k == KT - 1)
                    if k % 4 == 3:
                        ins.then_inc(s_pe, 1)

            def chunk2(b, x, k0, bank, first, last, jobs=0):
                for k in range(2):
                    split(b, k, jobs)
                    for t in range(KT):
                        ins = three(B[bank + t // 2][:, SEQ * (t % 2):SEQ * (t % 2) + SEQ], wslot(b), x,
                                    (A, slice(D * k + P * t, D * k + P * t + P)), (A, k0 + k, A), True,
                                    first and k == 0 and t % 2 == 0, last and k == 1)
                    ins.then_inc(s_pe, 1)

            def column_sum(bank, src, n, waits):
                for i in range(4):
                    waits(i)
                    for t in (2 * i, 2 * i + 1):
                        ins = mm(B[bank][:, 0:SEQ], ONES[:, :], src[:, t, :], start=t == 0, stop=t == KT - 1)
                return ins

            def sum_x(m):
                column_sum(7, ZSQ, m, lambda i: pe.wait_ge(s_xq, 4 * m + i + 1)).then_inc(s_xm, 1)

            pe.wait_ge(s_pool, 15)
            pe.wait_ge(s_ldx, 32)
            for n in range(4):
                for t in (2 * n, 2 * n + 1):
                    for b in range(BLK):
                        ins = nc.tensor.transpose(B[n][:, SEQ * (t % 2) + P * b:SEQ * (t % 2) + P * b + P],
                                                  XT[:, b, P * t:P * t + P], IDENT[:, :])
                ins.then_inc(s_tp, 1)
            pe.wait_ge(s_ld, 16 * N_LD)
            for layer in range(DEPTH):
                for k in range(PKT):
                    for b in range(BLK):
                        ins = nc.tensor.transpose(B[4 + layer][:, SEQ * k + P * b:SEQ * k + P * b + P],
                                                  PT[:, BLK * layer + b, P * k:P * k + P], IDENT[:, :])
                ins.then_inc(s_tp, 1)
            nc.tensor.transpose(B[6][:, 0:98], R1[:, :], IDENT[0:98, 0:98])
            nc.tensor.transpose(B[6][:, 128:256], R2[:, :], IDENT[:, :]).then_inc(s_tp, 1)

            def gate_products(layer, t):
                n = KT * layer + t
                if t % 2 == 0:
                    pe.wait_ge(s_u, 4 * layer + t // 2 + 1)
                if t == 0:
                    pe.wait_ge(s_bd, 64 * (layer + 1))
                if t >= 2:
                    pe.wait_ge(s_ga, n - 1)
                bank = B[3 if t % 2 == 0 else 7]
                for kind in range(2):
                    ins = mm(bank[:, SEQ * kind:SEQ * kind + SEQ], BD[:, kind, t, :], U[:, t % 4, :],
                             start=True, stop=True)
                ins.then_inc(s_gt, 1)

            def swap(layer, i):
                n = 8 * layer + i
                pe.wait_ge(s_eva, eva(layer, 8 + i))
                if i:
                    pe.wait_ge(s_qr, n)
                mm(B[6][:, :], SWAP[:, :], QT[:, i % 2, :, :], start=True, stop=True).then_inc(s_qs, 1)

            def scores(layer, h):
                n = HEADS * layer + h
                if h == 0:
                    pe.wait_ge(s_qr, 8 * layer + 8)
                else:
                    pe.wait_ge(s_mx, n)
                for m in range(2):
                    r = slice(HD * m, HD * m + HD)
                    mm(B[4 + m][:, 0:P], Q[r, h, 0:P], K[r, h, 0:P], start=True, stop=True)
                for m in range(2):
                    r = slice(HD * m, HD * m + HD)
                    ins = mm(B[4 + m][:, P:P + SEQ], Q[r, h, P:SEQ], K[r, h, :], start=True, stop=True)
                ins.then_inc(s_sc, 1)

            def turn(layer, h):
                n = HEADS * layer + h
                pe.wait_ge(s_df, n + 1)
                if h:
                    pe.wait_ge(s_wc, n)
                sc = SC[:, h % 2, :]
                for i, c in enumerate((0, SEQ, SEQ + P)):
                    ins = nc.tensor.transpose(B[6][:, P * i:P * i + P], sc[:, c:c + P], IDENT[:, :])
                ins.then_inc(s_wt, 1)

            def values(layer, h):
                n = HEADS * layer + h
                pe.wait_ge(s_wc, n + 1)
                if h:
                    pe.wait_ge(s_oc, n)
                else:
                    pe.wait_ge(s_eva, eva(layer, 19))
                c = slice(P * h, P * h + P)
                mm(B[7][:, 0:SEQ], V[:, 0, c], WT[:, h % 2, 0:SEQ], start=True, stop=False, skip_group_check=True)
                mm(B[7][:, P:SEQ], V[:, 1, c], WT[:, h % 2, SEQ:SEQ + P], start=False, stop=True,
                   skip_group_check=True).then_inc(s_o, 1)

            def head_square(layer, h):
                n = HEADS * layer + h
                pe.wait_ge(s_oc, n + 1)
                if h:
                    pe.wait_ge(s_oe, n)
                mm(B[3][:, 0:SEQ], ONES[:, :], OSQ[:, h % 2, :], start=True, stop=True).then_inc(s_om, 1)

            def mixer(layer):
                b = BASE[layer]
                for c in range(MIX):
                    if c >= 3:
                        if 28 <= c - 3 < 36:
                            pe.wait_ge(s_evd, evd(layer, c - 3))
                        else:
                            pe.wait_ge(s_eva, eva(layer, c - 3))
                    bank = c % 3
                    if 16 <= c < 20:
                        chunk8v(b + c, (HH, HL), bank)
                    elif c < 28:
                        ready = lambda k: pe.wait_ge(s_hl, 12 * layer + k // 2 + 1) if k % 2 == 0 else None
                        chunk8(b + c, (HH, HL), bank, ready if c == 0 else None)
                    elif c < 32:
                        if c == 28:
                            pe.wait_ge(s_ya, layer + 1)
                        chunk8(b + c, (YAH, YAL), bank)
                    elif c < 36:
                        ready = lambda k: pe.wait_ge(s_yb, 2 * layer + k // 4 + 1) if k % 4 == 0 else None
                        chunk8(b + c, (YBH, YBL), bank, ready if c == 32 else None)
                    else:
                        ready = lambda k: pe.wait_ge(s_ml, 4 * layer + k // 2 + 1) if k % 2 == 0 else None
                        chunk8(b + c, (YAH, YAL), bank, ready if c == 36 else None)
                    if c in (2, 3, 9, 10):
                        t = 2 * (c - 2) if c < 4 else 2 * (c - 7)
                        gate_products(layer, t)
                        gate_products(layer, t + 1)
                    if 9 <= c < 17:
                        swap(layer, c - 9)
                    if 18 <= c < 26:
                        scores(layer, c - 18)
                    if 20 <= c < 28:
                        turn(layer, c - 20)
                    if 21 <= c < 29:
                        values(layer, c - 21)
                    if 22 <= c < 30:
                        head_square(layer, c - 22)
                column_sum(3, ZSQ, 0, lambda i: pe.wait_ge(s_eva, eva(layer, 36 + i))).then_inc(s_zm, 1)

            def sum_z(z0):
                column_sum(3, ZSQ, 0, lambda i: pe.wait_ge(s_zq, z0 + i + 1)).then_inc(s_zm, 1)

            def embed(b, jobs, layer):
                pe.wait_ge(s_pl, layer + 1)
                pe.wait_ge(s_zs, 3 * layer + 2)
                chunk2(b, (PHI, PLO), 0, 0, True, True, jobs)

            def embed_gates(b, jobs, m, z0):
                for i in range(4):
                    ready = lambda k: pe.wait_ge(s_hl, 4 * m + k // 2 + 1) if k % 2 == 0 else None
                    chunk8(b + 1 + i, (HH, HL), 4 + i, ready if i == 0 else None, jobs)
                pe.wait_ge(s_pp, m // 3 + 1)
                sum_z(z0)

            sum_x(0)
            mixer(0)
            sum_x(1)

            def dense(s, it, q):
                b = FFN0 + 2 * q
                for n in range(2):
                    pe.wait_ge(f_a if n else f_s, s + 1)
                    chunk8(b + n, (HH, HL), 2 * (q % 2) + n, None, 0, it)

            pe.wait_ge(s_hl, 8)
            with pe.Fori(0, 2) as it:
                for q in range(6):
                    dense(6 * it + q, it, q)
            for q in range(2):
                dense(12 + q, 2, q)
            for d in range(14):
                b = FFN0 + GU + d
                pe.wait_ge(f_l, d + 1)
                chunk2(b, (FH, FL), 2 * d, 4, d == 0, d == 13)
            sum_z(0)
            embed(PLE0, 0, 0)
            sum_x(2)
            embed_gates(PLE0, 0, 2, 4)
            sum_x(3)
            mixer(1)
            sum_x(4)

            pe.wait_ge(s_hf, 4 * 5)
            for b in range(BLK):
                for k in range(KT):
                    ins = mm(B[0][:, EXPERTS * b:EXPERTS * b + EXPERTS], HF[:, k, P * b:P * b + P], RW[:, k, :],
                             start=k == 0, stop=k == KT - 1)
            ins.then_inc(r_lg, 1)
            for n in range(4):
                for t in range(4):
                    ins = nc.tensor.transpose(B[2 + n][:, P * t:P * t + P],
                                              HF[:, 4 * (n % 2) + t, P * (n // 2):P * (n // 2) + P], IDENT[:, :])
                ins.then_inc(r_tp, 1)
            pe.wait_ge(r_sel, 1)
            sel = (RT[:, 9, 0, :], RT[:, 9, 1, :])
            mm(B[1][:, 0:8], BEFORE[:, :], sel[0], start=True, stop=True)
            mm(B[1][:, 8:16], ONES[:, :], sel[0], start=True, stop=False)
            mm(B[1][:, 8:16], BEFORE[:, :], sel[1], start=False, stop=True)
            mm(B[1][:, 16:24], ONES[:, :], sel[0], start=True, stop=False)
            mm(B[1][:, 16:24], ONES[:, :], sel[1], start=False, stop=True).then_inc(r_rk, 1)

            def gather(u):
                src = HTH if u < 2 else HTL
                for i in range(4):
                    t = 4 * (u % 2) + i
                    for b in range(BLK):
                        ins = mm(B[7][:, P * i:P * i + P], src[:, b, P * t:P * t + P], DSEL[:, b, :],
                                 start=b == 0, stop=b == BLK - 1)
                ins.then_inc(m_p7, 1)

            def scatter(i):
                for t in (2 * i, 2 * i + 1):
                    ins = mm(B[7][:, SEQ * (t % 2):SEQ * (t % 2) + SEQ], Y[:, P * t:P * t + P], S[:, :],
                             start=True, stop=True)
                ins.then_inc(m_p7, 1)

            pe.wait_ge(m_d, 1)
            for u in range(4):
                if u == 0:
                    pe.wait_ge(r_th, 4)
                if u == 2:
                    pe.wait_ge(r_tl, 4)
                if u:
                    pe.wait_ge(m_b7, u)
                gather(u)
            pe.wait_ge(m_z, 3)
            pe.wait_ge(r_j, 1)
            jobs = pe.value_load(JINFO[0:1, 0:1], min_val=EXPERTS, max_val=MAX_JOBS)
            with pe.Fori(0, jobs) as j:
                for c in range(FFN):
                    b = MOE0 + c
                    if c == 0:
                        pe.wait_ge(m_b7, 4 + U7 * j)
                    if c < GU:
                        f, part = c // 4, c % 4
                        bank = 2 * (f % 2) + part // 2
                        if part % 2 == 0:
                            pe.wait_ge(m_a if part else m_s, 7 * j + (f + 1 if f else 2))
                        for k in range(4):
                            kt = 4 * (part % 2) + k
                            if k % 2 == 0:
                                split(b, k // 2, j)
                            ins = three(B[bank][:, :], wslot(b), (XGH, XGL), (A, slice(512 * k, 512 * k + 512)),
                                        (A, kt, A), False, kt == 0, kt == KT - 1)
                            if k % 2 == 1:
                                ins.then_inc(s_pe, 1)
                    else:
                        d = c - GU
                        if d == 0:
                            pe.wait_ge(m_y0, j + 1)
                            pe.wait_ge(m_y1, j + 1)
                        if d % 2 == 0:
                            pe.wait_ge(m_tl, 7 * j + 2 + d // 2)
                        for k in range(2):
                            split(b, k, j)
                            for h in range(2):
                                ins = three(B[4 + h][:, :], wslot(b), (ATH, ATL),
                                            (A, slice(D * k + 512 * h, D * k + 512 * h + 512)), (A, 2 * d + k, A),
                                            False, d == 0 and k == 0, d == 13 and k == 1)
                            ins.then_inc(s_pe, 1)
                    if c in SCATTER:
                        i = SCATTER.index(c)
                        if i == 0:
                            pe.wait_ge(m_y0, j + 1)
                            pe.wait_ge(m_y1, j + 1)
                        pe.wait_ge(m_b7, 4 + U7 * j + i)
                        scatter(i)
                    if c % 4 == 1 and 5 <= c < 30:
                        f = (c - 5) // 4
                        pe.wait_ge(m_a, 7 * j + f + 3)
                        pe.wait_ge(m_tl, 7 * j + f + 1)
                        for i in range(4):
                            ins = nc.tensor.transpose(B[6][:, P * i:P * i + P], MA[:, f % 2, P * i:P * i + P],
                                                      IDENT[:, :])
                        ins.then_inc(m_t, 1)
                    if c == TURN_W:
                        pe.wait_ge(m_dc, j + 1)
                        pe.wait_ge(m_b7, 4 + U7 * j + 4)
                        for t in range(BLK):
                            ins = nc.tensor.transpose(B[7][:, P * t:P * t + P], DC[:, t, :], IDENT[:, :])
                        ins.then_inc(m_p7, 1)
                    if c in GATHER:
                        u = GATHER.index(c)
                        pe.wait_ge(m_d, j + 2)
                        pe.wait_ge(m_b7, 4 + U7 * j + 5 + u)
                        gather(u)
            pe.wait_ge(m_y0, jobs + 1)
            pe.wait_ge(m_y1, jobs + 1)
            for i in range(4):
                pe.wait_ge(m_b7, 4 + U7 * jobs + i)
                scatter(i)
            sum_z(8)
            embed(MOE0, jobs, 1)
            sum_x(5)
            embed_gates(MOE0, jobs, 4, 12)
            for n in range(4):
                for t in range(4):
                    k = 4 * (n % 2) + t
                    pe.wait_ge(s_xn, 24 + k // 2 + 1)
                    ins = nc.tensor.transpose(B[n][:, P * t:P * t + P],
                                              XF[:, k, P * (n // 2):P * (n // 2) + P], IDENT[:, :])
                ins.then_inc(s_ot, 1)


_INS = ['x', 'p', 'positions', 'norm_g', 'w_in', 'conv_w', 'conv_b', 'lru_wa', 'lru_ba', 'lru_wx', 'lru_bx', 'lru_lam',
        'diff_lambda', 'subln_g', 'w_proj_a', 'w_proj_b', 'w_out', 'ffn_w_gate', 'ffn_w_up', 'ffn_w_down', 'router_w',
        'moe_w_gate', 'moe_w_up', 'moe_w_down', 'ple_w_proj', 'ple_w_gate']


def kernel(**inputs):
    import numpy as _np
    import concourse.bacc as _bacc
    from concourse import mybir as _mybir
    from concourse.bass_utils import run_bass_kernel_spmd as _run

    nc = _bacc.Bacc("TRN2", target_bir_lowering=False, num_devices=1)
    given = {name: _np.ascontiguousarray(inputs[name]) for name in _INS}
    freq = 10000.0 ** (-_np.arange(0, HD, 2, dtype=_np.float64) / HD)
    given['inv_freq'] = _np.tile(freq.astype(_np.float32), 4).reshape(P, 1)
    arrays, args = {}, []
    for name, a in given.items():
        arrays[f"in_{name}_dram"] = a
        args.append(nc.dram_tensor(f"in_{name}_dram", a.shape, _mybir.dt.from_np(a.dtype), kind="ExternalInput").ap())
    args.append(nc.dram_tensor("out_0_dram", (1, SEQ, D), F32, kind="ExternalOutput").ap())
    bass_hybrid_rglru_diffattn_moe(nc, *args)
    r = _run(nc, [arrays], core_ids=[0])
    return r.results[0]["out_0_dram"]
```

```python
import math
from contextlib import ExitStack

import numpy as np

import concourse.bass as bass
from concourse import mybir

ALU = mybir.AluOpType
ACT = mybir.ActivationFunctionType
AX = mybir.AxisListType
F32 = mybir.dt.float32
F32R = mybir.dt.float32r
I32 = mybir.dt.int32

P = 128
D = 1024
SEQ = 256
DEPTH = 2
KT = D // P
BLK = SEQ // P
PLE = 256
PKT = PLE // P
N_NORMS = 6
EPS = 1e-6
HEADS = 8
HD = 64
D_FF = 3584
FT = D_FF // P
EXPERTS = 8
NEG = -1e30
TOKENS = P
MAX_EXTRA = 3
MAX_JOBS = EXPERTS + MAX_EXTRA

CH = 2048
RAW = 6
HC = CH // 2
SPL = 3
MIX = 40
GU = 28
FFN = 42
PLEC = 5
BASE = (0, MIX + FFN + PLEC)
FFN0 = MIX
PLE0 = MIX + FFN
PLEP1 = BASE[1] + MIX
MOE0 = PLEP1 + 1
GROUP = (1, 2, 3, 4, 0, 5, 6)
N_LD0, N_LD1, N_LD2 = 2, 7, 3
U7 = 9
SCATTER = (1, 4, 8, 12)
TURN_W = 16
GATHER = (31, 33, 35, 37)
assert FFN % RAW == 0 and FFN % SPL == 0


def bass_hybrid_rglru_diffattn_moe(nc, x, p, positions, norm_g, w_in, conv_w, conv_b, lru_wa, lru_ba, lru_wx,
                                   lru_bx, lru_lam, diff_lambda, subln_g, w_proj_a, w_proj_b, w_out, ffn_w_gate,
                                   ffn_w_up, ffn_w_down, router_w, moe_w_gate, moe_w_up, moe_w_down, ple_w_proj,
                                   ple_w_gate, inv_freq, out):
    ctx = ExitStack()
    with ctx:
        base0 = 16512
        cursor = [base0]

        def at(name, off, shape, dt=F32):
            return nc.alloc_sbuf_tensor_at(name, shape, dt, offset=off)

        def keep(name, shape, dt=F32):
            off = cursor[0]
            size = 4 * int(np.prod(shape[1:]))
            cursor[0] = off + (size + 31) // 32 * 32
            return at(name, off, shape, dt)

        raw = [keep(f"raw{i}", [P, CH]) for i in range(RAW)]
        whi = [keep(f"whi{i}", [P, CH], F32R) for i in range(SPL)]
        wlo = [keep(f"wlo{i}", [P, CH], F32R) for i in range(SPL)]
        XF = keep("XF", [P, KT, SEQ])
        PF = keep("PF", [P, DEPTH, PKT, SEQ])
        IDENT = keep("IDENT", [P, P])
        SWAP = keep("SWAP", [P, P])
        ONES = keep("ONES", [P, P])
        BEFORE = keep("BEFORE", [P, P])
        IOTA = keep("IOTA", [P, P])
        MASK = keep("MASK", [P, SEQ])
        COS = keep("COS", [P, SEQ])
        SIN = keep("SIN", [P, SEQ])
        V1 = keep("V1", [P, 98])
        V2 = keep("V2", [P, P])
        SPLAM = keep("SPLAM", [P, DEPTH * KT])
        GSUB = keep("GSUB", [P, DEPTH])
        NLAM = keep("NLAM", [P, DEPTH])
        EPSC = keep("EPSC", [P, 1])
        RW = keep("RW", [P, KT, EXPERTS])
        STD = keep("STD", [P, SEQ])
        RINV = keep("RINV", [P, SEQ])
        RCOL = keep("RCOL", [P, BLK])
        JUNK = keep("JUNK", [P, 1])
        SM = keep("SM", [P, 160])
        RT = keep("RT", [P, 18, BLK, EXPERTS])
        AMX = keep("AMX", [P, 2, 4])
        ASUM = keep("ASUM", [P, 2, 4])
        AR = keep("AR", [P, 2, 4])
        JR = keep("JR", [P, BLK, MAX_JOBS + 1])
        JC = keep("JC", [P, BLK, MAX_JOBS + 1])
        JINFO = keep("JINFO", [P, 4], I32)
        arena = cursor[0]
        KB = 1024
        end = 229344

        a0 = arena
        HH = at("HH", a0, [P, KT, SEQ], F32R)
        HL = at("HL", a0 + 8 * KB, [P, KT, SEQ], F32R)
        o_rin = a0 + 16 * KB
        RIN = at("RIN", o_rin, [P, KT, SEQ + 3])
        o_bd = o_rin + 8 * KB + 128
        BD = at("BD", o_bd, [P, 2, KT, P])
        YAH = at("YAH", o_rin, [P, KT, SEQ], F32R)
        YAL = at("YAL", o_bd, [P, KT, SEQ], F32R)
        o_rt = o_bd + 8 * KB
        T2 = at("T2", o_rt, [P, KT, SEQ])
        IG = at("IG", o_rt + 8 * KB, [P, KT, SEQ])
        SC = at("SC", o_bd, [P, 2, 3 * SEQ])
        WT = at("WT", o_rt, [P, 2, 3 * P])
        OSQ = at("OSQ", o_rt + 8 * KB, [P, 2, SEQ])
        o_gel = o_rt + 16 * KB
        GEL = at("GEL", o_gel, [P, KT, SEQ])
        SGB = at("SGB", o_gel, [P, KT, SEQ])
        U = at("U", o_gel, [P, KT, SEQ])
        SQ = at("SQ", o_gel, [P, KT, SEQ])
        XSUM = at("XSUM", o_gel + KB, [P, SEQ])
        RINV2 = at("RINV2", o_gel, [P, SEQ])
        o_q = o_gel + 8 * KB
        Q = at("Q", o_q, [P, KT, SEQ])
        K = at("K", o_q + 8 * KB, [P, KT, SEQ])
        V = at("V", o_q + 16 * KB, [P, BLK, D])
        o_sga = o_q + 24 * KB
        SGA = at("SGA", o_sga, [P, KT, SEQ])
        QT = at("QT", o_sga, [P, 2, 2, SEQ])
        QS = at("QS", o_sga + 4 * KB, [P, 2, SEQ])
        COSR = at("COSR", o_sga + 6 * KB, [P, SEQ])
        SINR = at("SINR", o_sga + 7 * KB, [P, SEQ])
        top = o_sga + 8 * KB
        assert top <= end, (top, end)
        OALL, MSALL = Q, K
        YBH, YBL = HH, HL
        Z, ZSQ, HF = Q, K, at("HF", o_q + 16 * KB, [P, KT, SEQ])

        FH = at("FH", a0 + 16 * KB, [P, FT, SEQ], F32R)
        FL = at("FL", a0 + 44 * KB, [P, FT, SEQ], F32R)
        FS = at("FS", a0 + 72 * KB, [P, 2, 512])
        FA = at("FA", a0 + 76 * KB, [P, 2, 512])

        PP = (at("PP0", o_rt, [P, KT, SEQ]), at("PP1", o_q + 16 * KB, [P, KT, SEQ]))
        PG = at("PG", o_rt + 8 * KB, [P, 2, 512])
        PHI = at("PHI", o_rt + 12 * KB, [P, PKT, SEQ], F32R)
        PLO = at("PLO", o_rt + 14 * KB, [P, PKT, SEQ], F32R)

        HTH = at("HTH", a0, [P, BLK, D], F32R)
        HTL = at("HTL", a0 + 8 * KB, [P, BLK, D], F32R)
        XGH = at("XGH", a0 + 16 * KB, [P, KT, TOKENS], F32R)
        XGL = at("XGL", a0 + 20 * KB, [P, KT, TOKENS], F32R)
        ATH = at("ATH", a0 + 24 * KB, [P, FT, TOKENS], F32R)
        ATL = at("ATL", a0 + 38 * KB, [P, FT, TOKENS], F32R)
        MS = at("MS", a0 + 52 * KB, [P, 2, 512])
        FACC = at("FACC", o_q, [P, KT, SEQ])
        MA = at("MA", o_q + 8 * KB, [P, 2, 512])
        o_m = o_sga
        DSEL = at("DSEL", o_m, [P, BLK, TOKENS], F32R)
        DC = at("DC", o_m + 1 * KB, [P, BLK, TOKENS])
        S = at("S", o_m + 2 * KB, [P, SEQ])
        JT = at("JT", o_m + 3 * KB, [P, 2 + 2 * BLK, MAX_EXTRA, EXPERTS])
        Y = at("Y", o_m + 4 * KB, [P, D])
        assert a0 + 56 * KB <= o_q

        XT = at("XT", o_q, [P, BLK, D])
        PT = at("PT", o_rt, [P, DEPTH * BLK, PLE])
        R1 = at("R1", o_rt + 4 * KB, [98, P])
        R2 = at("R2", o_rt + 5 * KB, [P, P])
        DL = at("DL", o_rt + 6 * KB, [P, DEPTH * 4, HD])
        POSI = at("POSI", o_gel, [P, SEQ], I32)
        POSF = at("POSF", o_gel + KB, [P, SEQ])
        TT = at("TT", o_gel + 2 * KB, [P, 4, SEQ])
        IFR = at("IFR", o_gel + 6 * KB, [P, 1])
        OT = at("OT", a0, [P, BLK, D])

        B = [ctx.enter_context(nc.psum_tensor(f"bank{i}", [P, 512], F32)) for i in range(8)]

        def sem(name):
            return ctx.enter_context(nc.semaphore(name))

        s_w = [sem(f"s_w{i}") for i in range(RAW)]
        s_hi = sem("s_hi")
        s_lo = sem("s_lo")
        s_pe = sem("s_pe")
        s_ld0 = sem("s_ld0")
        s_ld1 = sem("s_ld1")
        s_ld2 = sem("s_ld2")
        s_ldx = sem("s_ldx")
        s_bd = sem("s_bd")
        s_bdz = sem("s_bdz")
        s_pool = sem("s_pool")
        s_ac = sem("s_ac")
        s_dc = sem("s_dc")
        s_tp = sem("s_tp")
        s_tc = sem("s_tc")
        s_r0 = sem("s_r0")
        s_r1 = sem("s_r1")
        s_c0 = sem("s_c0")
        s_c1 = sem("s_c1")
        s_c2 = sem("s_c2")
        s_eva = sem("s_eva")
        s_evd = sem("s_evd")
        s_u = sem("s_u")
        s_gt = sem("s_gt")
        s_ga = sem("s_ga")
        s_sq = sem("s_sq")
        s_iu = sem("s_iu")
        s_den = sem("s_den")
        s_bl = sem("s_bl")
        s_al = sem("s_al")
        s_ri = sem("s_ri")
        s_rt = sem("s_rt")
        s_rc = sem("s_rc")
        s_ge = sem("s_ge")
        s_tg = sem("s_tg")
        s_y = sem("s_y")
        s_yh = sem("s_yh")
        s_ya = sem("s_ya")
        s_qs = sem("s_qs")
        s_qr = sem("s_qr")
        s_sc = sem("s_sc")
        s_mx = sem("s_mx")
        s_ex = sem("s_ex")
        s_df = sem("s_df")
        s_wt = sem("s_wt")
        s_wc = sem("s_wc")
        s_o = sem("s_o")
        s_oc = sem("s_oc")
        s_om = sem("s_om")
        s_oe = sem("s_oe")
        s_or = sem("s_or")
        s_os = sem("s_os")
        s_yf = sem("s_yf")
        s_ybh = sem("s_ybh")
        s_yb = sem("s_yb")
        s_m = sem("s_m")
        s_mh = sem("s_mh")
        s_ml = sem("s_ml")
        s_zq = sem("s_zq")
        s_zp = sem("s_zp")
        s_zm = sem("s_zm")
        s_zs = sem("s_zs")
        s_xn = sem("s_xn")
        s_xq = sem("s_xq")
        s_xr = sem("s_xr")
        s_xm = sem("s_xm")
        s_xs = sem("s_xs")
        s_hf = sem("s_hf")
        s_hh = sem("s_hh")
        s_hl = sem("s_hl")
        f_g = sem("f_g")
        f_u = sem("f_u")
        f_s = sem("f_s")
        f_a = sem("f_a")
        f_h = sem("f_h")
        f_l = sem("f_l")
        s_ph = sem("s_ph")
        s_pl = sem("s_pl")
        s_pp = sem("s_pp")
        s_pr = sem("s_pr")
        s_pg = sem("s_pg")
        r_lg = sem("r_lg")
        r_d = sem("r_d")
        r_e = sem("r_e")
        r_sel = sem("r_sel")
        r_rk = sem("r_rk")
        r_j = sem("r_j")
        r_tp = sem("r_tp")
        r_th = sem("r_th")
        r_tl = sem("r_tl")
        m_z = sem("m_z")
        m_s = sem("m_s")
        m_a = sem("m_a")
        m_t = sem("m_t")
        m_th = sem("m_th")
        m_tl = sem("m_tl")
        m_d = sem("m_d")
        m_dc = sem("m_dc")
        m_p7 = sem("m_p7")
        m_b7 = sem("m_b7")
        m_y0 = sem("m_y0")
        m_y1 = sem("m_y1")
        s_ot = sem("s_ot")
        s_oo = sem("s_oo")
        s_out = sem("s_out")

        def eva(layer, c):
            return 16 * layer + (c - 3 if c < 16 else c - 23)

        def evd(layer, c):
            return 24 * layer + (c + 1 if c < 4 else c - 11)

        def by_scalar(c):
            return 4 <= c < 16 or c >= 36

        def rows(w):
            return w.rearrange("(k p) n -> p k n", p=P)

        block = ctx.enter_context(nc.Block())

        BY_TILES = (1, 2, 5)
        R_BANK = (6, 7, 3, 6)
        G_BANK = (7, 6, 3, 7)
        PP_BANK = ((0, 1, 2, 3), (0, 1, 2, 4))

        @block.sync
        def _(sp):
            def load(b, jobs, src, k):
                if isinstance(jobs, int) and b + FFN * jobs < RAW:
                    pass
                else:
                    sp.wait_ge(s_lo, 2 * (b - RAW + 1) + 2 * FFN * jobs)
                sp.dma_start(raw[b % RAW][:, :].rearrange("p (k n) -> p k n", k=k), src).then_inc(s_w[b % RAW], 16)

            def mixer(layer):
                b = BASE[layer]
                wi = rows(w_in[layer])
                for c in range(28):
                    if layer == 0 and c == 1:
                        sp.wait_ge(s_ld1, 16 * N_LD1)
                    if layer == 0 and c == 2:
                        sp.dma_start(DL[:, :, :],
                                     diff_lambda.rearrange("l j d -> (l j) d").partition_broadcast(P)).then_inc(s_ld2, 16)
                        sp.dma_start(PT[:, :, :], p.rearrange("l b (k t) d -> t (l b k) d", t=P)).then_inc(s_ld2, 16)
                        sp.dma_start(RW[:, :, :], rows(router_w[0])).then_inc(s_ld2, 16)
                    col = GROUP[c // 4] * D + (c % 4) * 256
                    load(b + c, 0, wi[:, :, col:col + 256], 8)
                for n, w in enumerate((w_proj_a, w_proj_b, w_out)):
                    for c in range(4):
                        load(b + 28 + 4 * n + c, 0, rows(w[layer])[:, :, 256 * c:256 * c + 256], 8)

            def embed(b, layer):
                load(b, 0, rows(ple_w_proj[layer]), 2)

            def embed_gates(b, jobs, layer):
                for c in range(4):
                    load(b + c, jobs, rows(ple_w_gate[layer])[:, :, 256 * c:256 * c + 256], 8)

            def expert(jobs, e):
                wg, wu, wd = (w[0, bass.ds(e, 1)].rearrange("a (k p) n -> p (a k) n", p=P)
                              for w in (moe_w_gate, moe_w_up, moe_w_down))
                for f in range(7):
                    for n, w in enumerate((wg, wu)):
                        for h in range(2):
                            load(MOE0 + 4 * f + 2 * n + h, jobs, w[:, 4 * h:4 * h + 4, 512 * f:512 * f + 512], 4)
                for d in range(14):
                    load(MOE0 + GU + d, jobs, wd[:, 2 * d:2 * d + 2, :], 2)

            for blk in range(BLK):
                sp.dma_start(XT[:, blk, :], x[0, P * blk:P * blk + P, :]).then_inc(s_ldx, 16)
            sp.dma_start(POSI[:, :], positions.partition_broadcast(P)[:, 0, :]).then_inc(s_ld0, 16)
            sp.dma_start(IFR[:, :], inv_freq).then_inc(s_ld0, 16)
            mixer(0)
            gate, up = rows(ffn_w_gate[0]), rows(ffn_w_up[0])
            for s in range(2):
                load(FFN0 + 2 * s, 0, gate[:, :, 256 * s:256 * s + 256], 8)
                load(FFN0 + 2 * s + 1, 0, up[:, :, 256 * s:256 * s + 256], 8)
            with sp.Fori(0, 2) as it:
                for s in range(2, 8):
                    for n, w in enumerate((gate, up)):
                        b = FFN0 + 2 * s + n
                        sp.wait_ge(s_lo, 2 * (b - RAW + 1) + 24 * it)
                        sp.dma_start(raw[b % RAW][:, :].rearrange("p (k n) -> p k n", k=8),
                                     w[:, :, bass.ds(it * 1536 + 256 * s, 256)]).then_inc(s_w[b % RAW], 16)
            for d in range(14):
                load(FFN0 + GU + d, 0, rows(ffn_w_down[0])[:, 2 * d:2 * d + 2, :], 2)
            embed(PLE0, 0)
            embed_gates(PLE0 + 1, 0, 0)
            mixer(1)
            embed(PLEP1, 1)
            with sp.Fori(0, EXPERTS) as j:
                expert(j, j)
            sp.wait_ge(r_j, 1)
            jobs = sp.value_load(JINFO[0:1, 0:1], min_val=EXPERTS, max_val=MAX_JOBS)
            for extra in range(MAX_EXTRA):
                with sp.If(jobs > EXPERTS + extra):
                    e = sp.value_load(JINFO[0:1, 1 + extra:2 + extra], min_val=0, max_val=EXPERTS - 1)
                    expert(EXPERTS + extra, e)
            embed_gates(MOE0, jobs, 1)
            for blk in range(BLK):
                sp.wait_ge(s_oo, 2 * blk + 2)
                sp.dma_start(out[0, P * blk:P * blk + P, :], OT[:, blk, :]).then_inc(s_out, 16)
            sp.wait_ge(s_out, 16 * BLK)

        @block.gpsimd
        def _(pool):
            pool.memset(IDENT[:, :], 0.0).then_inc(s_pool, 1)
            pool.memset(SWAP[:, :], 0.0).then_inc(s_pool, 1)
            pool.memset(ONES[:, :], 1.0).then_inc(s_pool, 1)
            pool.memset(BEFORE[:, :], 1.0).then_inc(s_pool, 1)
            pool.memset(MASK[:, :], 0.0).then_inc(s_pool, 1)
            pool.memset(EPSC[:, :], EPS).then_inc(s_pool, 1)
            pool.memset(RIN[:, :, 0:3], 0.0).then_inc(s_pool, 1)
            pool.memset(JR[:, :, EXPERTS:], -1.0).then_inc(s_pool, 1)
            pool.memset(JC[:, :, EXPERTS:], 0.0).then_inc(s_pool, 1)
            pool.memset(BD[:, :, :, :], 0.0).then_inc(s_bdz, 1)
            pool.iota(IOTA[:, :], [[1, P]], base=0, channel_multiplier=0,
                      allow_small_or_imprecise_dtypes=True).then_inc(s_pool, 1)
            pool.wait_ge(s_pool, 10)
            pool.affine_select(out=IDENT[:, :], in_=IDENT[:, :], compare_op=ALU.not_equal, fill=1.0, base=0,
                               pattern=[[-1, P]], channel_multiplier=1).then_inc(s_pool, 1)
            sw = SWAP[:, :].rearrange("p (g h j) -> p g h j", g=2, h=2)
            pool.affine_select(out=sw[:, :, 0, :], in_=sw[:, :, 0, :], compare_op=ALU.not_equal, fill=-1.0, base=-32,
                               pattern=[[-64, 2], [-1, 32]], channel_multiplier=1).then_inc(s_pool, 1)
            pool.affine_select(out=sw[:, :, 1, :], in_=sw[:, :, 1, :], compare_op=ALU.not_equal, fill=1.0, base=0,
                               pattern=[[-64, 2], [-1, 32]], channel_multiplier=1).then_inc(s_pool, 1)
            pool.affine_select(out=BEFORE[:, :], in_=BEFORE[:, :], compare_op=ALU.is_gt, fill=0.0, base=0,
                               pattern=[[1, P]], channel_multiplier=-1).then_inc(s_pool, 1)
            pool.affine_select(out=MASK[:, P:SEQ], in_=MASK[:, P:SEQ], compare_op=ALU.is_ge, fill=NEG, base=0,
                               pattern=[[-1, P]], channel_multiplier=1).then_inc(s_pool, 1)

            def gates(layer):
                for kind, w in enumerate((lru_wa, lru_wx)):
                    pairs = w[layer].rearrange("(t h) c d -> h c t d", h=2)
                    for h in range(2):
                        pool.dma_start(BD[HD * h:HD * h + HD, kind, :, HD * h:HD * h + HD], pairs[h]).then_inc(s_bd, 16)

            pool.wait_ge(s_bdz, 1)
            gates(0)
            pool.wait_ge(s_pe, 2 * (PLE0 + 1))
            pool.memset(BD[:, :, :, :], 0.0).then_inc(s_bdz, 1)
            pool.memset(RIN[:, :, 0:3], 0.0).then_inc(s_bdz, 1)
            pool.wait_ge(s_bdz, 3)
            gates(1)
            pool.wait_ge(s_hf, 4)
            pool.memset(FACC[:, :, :], 0.0).then_inc(m_z, 1)
            pool.memset(Y[:, :], 0.0).then_inc(m_z, 1)
            pool.memset(S[:, :], 0.0).then_inc(m_z, 1)

        @block.scalar
        def _(act):
            chain = [0]

            def link(ins):
                chain[0] += 1
                ins.then_inc(s_ac, 1)
                act.wait_ge(s_ac, chain[0])

            for s, n in ((m_s, 2), (m_y0, 1)):
                act.sem_inc(s, n)

            def load(dst, src, s):
                act.dma_start(dst, src).then_inc(s, 16)

            load(R1[0:96, :], norm_g.rearrange("l n (t p) -> (l n t) p", p=P), s_ld1)
            load(R1[96:98, :], subln_g, s_ld1)
            at_row = 0
            for v in (conv_w.rearrange("l j (t p) -> (l j t) p", p=P), conv_b.rearrange("l (t p) -> (l t) p", p=P),
                      lru_ba.rearrange("l (t p) -> (l t) p", p=P), lru_bx.rearrange("l (t p) -> (l t) p", p=P),
                      lru_lam.rearrange("l (t p) -> (l t) p", p=P)):
                n = v.shape[0]
                load(R2[at_row:at_row + n, :], v, s_ld1)
                at_row += n

            def hi(b, jobs=0):
                act.wait_ge(s_w[b % RAW], 16 * (b // RAW + 1) + 16 * (FFN // RAW) * jobs)
                for e in range(2):
                    if not (isinstance(jobs, int) and b + FFN * jobs < SPL):
                        act.wait_ge(s_pe, 2 * (b - SPL) + e + 1 + 2 * FFN * jobs)
                    r = slice(HC * e, HC * e + HC)
                    nc.scalar.activation(whi[b % SPL][:, r], raw[b % RAW][:, r], ACT.Copy).then_inc(s_hi, 1)

            def gcol(layer, n, t):
                i = (layer * N_NORMS + n) * KT + t
                return V1[:, i:i + 1]

            def squares(m):
                for i in range(4):
                    act.wait_ge(s_xn, 4 * m + i + 1)
                    nc.scalar.activation(ZSQ[:, 2 * i:2 * i + 2, :], XF[:, 2 * i:2 * i + 2, :],
                                         ACT.Square).then_inc(s_xq, 1)

            def gained(m):
                layer, n = m // 3, 2 * (m % 3)
                for i in range(4):
                    act.wait_ge(s_xn, 4 * m + i + 1)
                    for t in (2 * i, 2 * i + 1):
                        ins = nc.scalar.activation(HH[:, t, :], XF[:, t, :], ACT.Copy, scale=gcol(layer, n, t))
                    ins.then_inc(s_hh, 1)

            def root(m):
                act.wait_ge(s_xm, m + 1)
                nc.scalar.activation(STD[:, :], B[7][:, 0:SEQ], ACT.Sqrt, bias=EPSC[:, 0:1],
                                     scale=1.0 / D).then_inc(s_xs, 1)

            for n in range(4):
                act.wait_ge(s_tp, n + 1)
                nc.scalar.activation(XF[:, 2 * n:2 * n + 2, :], B[n][:, :].rearrange("p (t s) -> p t s", t=2),
                                     ACT.Copy).then_inc(s_xn, 1)
            hi(0)
            act.wait_ge(s_r0, 1)
            nc.scalar.activation(SIN[:, :], TT[:, 0, :], ACT.Sin).then_inc(s_r1, 1)
            nc.scalar.activation(COS[:, :], TT[:, 1, :], ACT.Sin).then_inc(s_r1, 1)
            act.wait_ge(s_tp, 5)
            nc.scalar.activation(V1[:, :], B[6][:, 0:98], ACT.Copy).then_inc(s_tc, 1)
            nc.scalar.activation(V2[:, :], B[6][:, 128:256], ACT.Copy).then_inc(s_tc, 1)
            act.wait_ge(s_tc, 2)
            gained(0)
            squares(0)
            for b in range(1, SPL):
                hi(b)

            def constants():
                act.wait_ge(s_c0, 1)
                nc.scalar.activation(SM[:, 0:16], SM[:, 16:32], ACT.Exp).then_inc(s_c1, 1)
                nc.scalar.activation(SM[:, 64:68], SM[:, 68:72], ACT.Exp).then_inc(s_c1, 1)
                for n in range(2):
                    act.wait_ge(s_tp, 6 + n)
                    nc.scalar.activation(PF[:, n, :, :], B[4 + n][:, :].rearrange("p (t s) -> p t s", t=2),
                                         ACT.Copy).then_inc(s_tc, 1)

            def sqrt_set():
                nc.scalar.activation(JUNK[:, :], EPSC[:, :], ACT.Sqrt)

            def postnorm(n, bank=3):
                if n != 1:
                    sqrt_set()
                act.wait_ge(s_zm, n + 1)
                nc.scalar.activation(STD[:, :], B[bank][:, 0:SEQ], ACT.Sqrt, bias=EPSC[:, 0:1],
                                     scale=1.0 / D).then_inc(s_zs, 1)

            def pair(t, i):
                return t[:, 2 * i:2 * i + 2, :]

            def bank2(n):
                return B[n][:, :].rearrange("p (t s) -> p t s", t=2)

            def gate_functions(layer, j):
                for t in (2 * j, 2 * j + 1):
                    act.wait_ge(s_gt, KT * layer + t + 1)
                    bank = B[3 if t % 2 == 0 else 7]
                    col = layer * KT + t
                    link(nc.scalar.activation(T2[:, t, :], bank[:, 0:SEQ], ACT.Sigmoid, bias=V2[:, 80 + col:81 + col]))
                    nc.scalar.activation(IG[:, t, :], bank[:, SEQ:], ACT.Sigmoid, bias=V2[:, 96 + col:97 + col])
                    if layer == 0 and t == 0:
                        act.wait_ge(s_c2, 1)
                    ins = nc.scalar.activation(T2[:, t, :], T2[:, t, :], ACT.Tanh, scale=SPLAM[:, col:col + 1])
                    ins.then_inc(s_ga, 1)

            def mixer(layer):
                b = BASE[layer]
                for c in range(MIX):
                    if c < MIX - 1:
                        hi(b + c + SPL)
                    if c == 0:
                        root(3 * layer)
                    if c == 1 and layer == 0:
                        constants()
                    if 4 <= c < 12:
                        i = c - 4
                        n = 8 * layer + i
                        if i >= 2:
                            act.wait_ge(s_qr, n - 1)
                        nc.scalar.activation(QT[:, i % 2, :, :], bank2(c % 3), ACT.Copy).then_inc(s_eva, 1)
                    elif 12 <= c < 16:
                        if c == 12:
                            act.wait_ge(s_rc, layer + 1)
                        for k in range(BLK):
                            ins = nc.scalar.activation(V[:, k, 256 * (c - 12):256 * (c - 11)],
                                                       B[c % 3][:, 256 * k:256 * k + 256], ACT.Copy,
                                                       scale=RCOL[:, k:k + 1])
                        ins.then_inc(s_eva, 1)
                    elif c == 20:
                        act.wait_ge(s_evd, evd(layer, 19))
                        nc.scalar.activation(GEL[:, :, :], GEL[:, :, :], ACT.Gelu_apprx_tanh).then_inc(s_ge, 1)
                    elif c == 22:
                        act.wait_ge(s_y, layer + 1)
                        nc.scalar.activation(YAH[:, :, :], GEL[:, :, :], ACT.Copy).then_inc(s_yh, 1)
                    elif c >= 36:
                        i = c - 36
                        if c == MIX - 1:
                            act.wait_ge(s_pe, 2 * (b + MIX))
                        nc.scalar.activation(pair(Z, i), bank2(c % 3), ACT.Copy)
                        nc.scalar.activation(pair(ZSQ, i), bank2(c % 3), ACT.Square).then_inc(s_eva, 1)
                        if c == MIX - 1:
                            hi(b + c + SPL)
                    if 2 <= c < 6:
                        gate_functions(layer, c - 2)
                    if c == 6:
                        act.wait_ge(s_ga, KT * (layer + 1))
                        act.wait_ge(s_iu, layer + 1)
                        nc.scalar.activation(SQ[:, :, :], T2[:, :, :], ACT.Sqrt).then_inc(s_sq, 1)
                    if c == 7:
                        nc.scalar.activation(T2[:, :, :], T2[:, :, :], ACT.Copy, bias=1.0).then_inc(s_den, 1)
                    if c in (12, 16):
                        g = (c - 12) // 4
                        act.wait_ge(s_bl, KT * layer + 4 * g + 4)
                        r = T2[:, 4 * g:4 * g + 4, :]
                        nc.scalar.activation(r, r, ACT.Copy, bias=-1.0, scale=2.0).then_inc(s_al, 1)
                    h = c - 14
                    if 0 <= h < HEADS:
                        n = HEADS * layer + h
                        act.wait_ge(s_mx, n + 1)
                        sc, q = SC[:, h % 2, :], h % 2
                        for m in range(2):
                            nc.scalar.activation(sc[:, P * m:P * m + P], sc[:, P * m:P * m + P], ACT.Exp,
                                                 bias=AMX[:, q, m:m + 1], scale=HD ** -0.5,
                                                 accum_out=ASUM[:, q, m:m + 1])
                        for m in range(2):
                            r = sc[:, SEQ * (m + 1):SEQ * (m + 2)]
                            ins = nc.scalar.activation(r, r, ACT.Exp, bias=AMX[:, q, 2 + m:3 + m], scale=HD ** -0.5,
                                                       accum_out=ASUM[:, q, 2 + m:3 + m])
                        ins.then_inc(s_ex, 1)
                    if 21 <= c < 29:
                        i = c - 21
                        dst = pair(SGA, i) if i < 4 else pair(SGB, i - 4)
                        act.wait_ge(s_evd, evd(layer, c - 1))
                        nc.scalar.activation(dst, dst, ACT.Tanh, scale=0.5).then_inc(s_tg, 1)
                    h = c - 16
                    if 0 <= h < HEADS:
                        n = HEADS * layer + h
                        act.wait_ge(s_wt, n + 1)
                        if h >= 2:
                            act.wait_ge(s_o, n - 1)
                        nc.scalar.activation(WT[:, h % 2, :], B[6][:, 0:384], ACT.Copy).then_inc(s_wc, 1)
                    h = c - 17
                    if 0 <= h < HEADS:
                        n = HEADS * layer + h
                        act.wait_ge(s_o, n + 1)
                        if h >= 2:
                            act.wait_ge(s_om, n - 1)
                        nc.scalar.activation(OALL[:, h, :], B[7][:, 0:SEQ], ACT.Copy)
                        nc.scalar.activation(OSQ[:, h % 2, :], B[7][:, 0:SEQ], ACT.Square).then_inc(s_oc, 1)
                    h = c - 18
                    if 0 <= h < HEADS:
                        n = HEADS * layer + h
                        act.wait_ge(s_om, n + 1)
                        nc.scalar.activation(MSALL[:, h, :], B[3][:, 0:SEQ], ACT.Copy, bias=EPS,
                                             scale=1.0 / P).then_inc(s_oe, 1)
                    if c == 28:
                        act.wait_ge(s_or, HEADS * (layer + 1))
                        for g in range(2):
                            r = MSALL[:, 4 * g:4 * g + 4, :]
                            nc.scalar.activation(r, r, ACT.Sqrt).then_inc(s_os, 1)
                    if c in (29, 30):
                        g = c - 29
                        act.wait_ge(s_yf, 2 * layer + g + 1)
                        nc.scalar.activation(YBH[:, 4 * g:4 * g + 4, :], OALL[:, 4 * g:4 * g + 4, :],
                                             ACT.Copy).then_inc(s_ybh, 1)
                    if 32 <= c < 36:
                        i = c - 32
                        act.wait_ge(s_m, 4 * layer + i + 1)
                        nc.scalar.activation(pair(YAH, i), pair(SGB, i), ACT.Copy, scale=0.5).then_inc(s_mh, 1)

            def split_p(layer):
                nc.scalar.activation(PHI[:, :, :], PF[:, layer, :, :], ACT.Copy).then_inc(s_ph, 1)

            def embed(b, layer):
                hi(b + SPL)
                for n in range(4):
                    ins = nc.scalar.activation(pair(PP[layer], n), bank2(PP_BANK[layer][n]), ACT.Copy)
                ins.then_inc(s_pp, 1)

            def embed_gates(b, jobs, layer, z0):
                for i in range(4):
                    if i == 0:
                        hi(b + i + SPL, jobs)
                        root(3 * layer + 2)
                    act.wait_ge(s_pr, 4 * layer + i + 1)
                    nc.scalar.activation(PG[:, i % 2, :], PG[:, i % 2, :], ACT.Sigmoid).then_inc(s_pg, 1)
                    square_z(z0 + i + 1, i, Z)
                    if i > 0 and not layer:
                        hi(b + i + SPL)

            def square_z(n, i, z):
                act.wait_ge(s_zp, n)
                nc.scalar.activation(pair(ZSQ, i), pair(z, i), ACT.Square).then_inc(s_zq, 1)

            mixer(0)
            postnorm(0)
            gained(1)
            squares(1)

            def dense(s, b, it):
                for n in range(2):
                    nb = b + n + SPL
                    act.wait_ge(s_w[nb % RAW], 16 * (nb // RAW + 1) + 32 * it)
                    for e in range(2):
                        act.wait_ge(s_pe, 2 * (b + n) + e + 1 + 24 * it)
                        r = slice(HC * e, HC * e + HC)
                        nc.scalar.activation(whi[nb % SPL][:, r], raw[nb % RAW][:, r], ACT.Copy).then_inc(s_hi, 1)
                    if n == 0 and isinstance(s, int) and s == 0:
                        root(1)
                q = (b - FFN0) // 2 % 2
                act.wait_ge(f_g, s + 3)
                nc.scalar.activation(FS[:, q, :], FS[:, q, :], ACT.Silu).then_inc(f_s, 1)
                act.wait_ge(f_a, s + 3)
                nc.scalar.activation(FH[:, bass.ds(2 * s, 2), :] if not isinstance(s, int) else pair(FH, s),
                                     FA[:, q, :].rearrange("p (t s) -> p t s", t=2), ACT.Copy).then_inc(f_h, 1)

            for s in range(2):
                dense(s, FFN0 + 2 * s, 0)
            with act.Fori(0, 2) as it:
                nc.scalar.activation(JUNK[:, :], EPSC[:, :], ACT.Silu)
                for q in range(2, 8):
                    dense(6 * it + q, FFN0 + 2 * q, it)
            for d in range(13):
                hi(FFN0 + GU + d + SPL)
            split_p(0)
            sqrt_set()
            for i in range(4):
                square_z(i + 1, i, Z)
            hi(FFN0 + GU + 13 + SPL)
            postnorm(1, 4)
            gained(2)
            squares(2)
            embed(PLE0, 0)
            embed_gates(PLE0 + 1, 0, 0, 4)
            postnorm(2)
            gained(3)
            squares(3)
            mixer(1)
            split_p(1)
            postnorm(3)
            squares(4)
            root(4)
            nc.scalar.activation(JUNK[:, :], EPSC[:, :], ACT.Exp)

            for n in range(4):
                if n == 3:
                    act.wait_ge(r_d, 1)
                    nc.scalar.activation(SM[:, 52:54], SM[:, 50:52], ACT.Exp).then_inc(r_e, 1)
                act.wait_ge(r_tp, n + 1)
                nc.scalar.activation(HTH[:, n // 2, 512 * (n % 2):512 * (n % 2) + 512], B[R_BANK[n]][:, :],
                                     ACT.Copy).then_inc(r_th, 1)
            for u in range(2):
                act.wait_ge(m_p7, u + 1)
                nc.scalar.activation(XGH[:, 4 * u:4 * u + 4, :], B[G_BANK[u]][:, :].rearrange("p (t s) -> p t s", t=4),
                                     ACT.Copy).then_inc(m_b7, 1)
            embed(PLEP1, 1)
            act.wait_ge(r_j, 1)
            jobs = act.value_load(JINFO[0:1, 0:1], min_val=EXPERTS, max_val=MAX_JOBS)
            with act.Fori(0, jobs) as j:
                nc.scalar.activation(JUNK[:, :], EPSC[:, :], ACT.Silu)
                for c in range(FFN):
                    if c == FFN - 1:
                        act.wait_ge(s_pe, 2 * (MOE0 + FFN) + 2 * FFN * j)
                        nc.scalar.activation(Y[:, 0:512], B[4][:, :], ACT.Copy).then_inc(m_y0, 1)
                    hi(MOE0 + c + SPL, j)
                    if c < GU and c % 4 == 1:
                        f = c // 4
                        act.wait_ge(m_a, 7 * j + (f + 1 if f else 2))
                        nc.scalar.activation(MS[:, f % 2, :], B[2 * (f % 2)][:, :], ACT.Silu).then_inc(m_s, 1)
                    if c % 4 == 2 and 6 <= c <= 30:
                        f = (c - 6) // 4
                        act.wait_ge(m_t, 7 * j + f + 1)
                        nc.scalar.activation(ATH[:, 4 * f:4 * f + 4, :], B[6][:, :].rearrange("p (t s) -> p t s", t=4),
                                             ACT.Copy).then_inc(m_th, 1)
                    if c in GATHER[:2]:
                        u = GATHER.index(c)
                        act.wait_ge(m_p7, 4 + U7 * j + 5 + u + 1)
                        nc.scalar.activation(XGH[:, 4 * u:4 * u + 4, :],
                                             B[7][:, :].rearrange("p (t s) -> p t s", t=4), ACT.Copy).then_inc(m_b7, 1)
            for i in range(4):
                square_z(8 + i + 1, i, FACC)
            postnorm(4, 4)
            gained(5)
            squares(5)
            embed_gates(MOE0, jobs, 1, 12)
            postnorm(5)
            for n in range(4):
                act.wait_ge(s_ot, n + 1)
                nc.scalar.activation(OT[:, n // 2, 512 * (n % 2):512 * (n % 2) + 512], B[n][:, :],
                                     ACT.Copy).then_inc(s_oo, 1)


        @block.vector
        def _(dve):
            chain = [0]

            def mark(ins):
                chain[0] += 1
                ins.then_inc(s_dc, 1)
                return chain[0]

            def link(ins):
                dve.wait_ge(s_dc, mark(ins))

            v = nc.vector

            def pair(t, i):
                return t[:, 2 * i:2 * i + 2, :]

            def bank2(n):
                return B[n][:, :].rearrange("p (t s) -> p t s", t=2)

            def lo(b, jobs=0):
                for e in range(2):
                    dve.wait_ge(s_hi, 2 * b + e + 1 + 2 * FFN * jobs)
                    r = slice(HC * e, HC * e + HC)
                    v.tensor_tensor(wlo[b % SPL][:, r], raw[b % RAW][:, r], whi[b % SPL][:, r].bitcast(F32),
                                    ALU.subtract).then_inc(s_lo, 1)

            for s, n in ((f_g, 2), (f_a, 2), (m_a, 2), (m_tl, 1), (m_y1, 1)):
                dve.sem_inc(s, n)

            def gcol(layer, n, t):
                i = (layer * N_NORMS + n) * KT + t
                return V1[:, i:i + 1]

            def gained(m):
                layer, n = m // 3, 2 * (m % 3)
                if m == 0:
                    dve.wait_ge(s_tc, 2)
                for i in range(4):
                    dve.wait_ge(s_hh, 4 * (m if m < 4 else m - 1) + i + 1)
                    for t in (2 * i, 2 * i + 1):
                        ins = v.scalar_tensor_tensor(out=HL[:, t, :], in0=XF[:, t, :], scalar=gcol(layer, n, t),
                                                     in1=HH[:, t, :].bitcast(F32), op0=ALU.mult, op1=ALU.subtract)
                    ins.then_inc(s_hl, 1)

            def sum_tiles(m):
                dve.wait_ge(s_xq, 4 * m + 4)
                v.tensor_reduce(XSUM[:, :], ZSQ[:, :, :].rearrange("p t s -> p s t"), AX.X, ALU.add).then_inc(s_xr, 1)

            def inverse(m):
                dve.wait_ge(s_xs, m + 1)
                link(v.reciprocal(RINV[:, :], STD[:, :]))

            def scaled(dst, src):
                return v.tensor_tensor(dst, src, RINV[:, :].unsqueeze(1).to_broadcast([P, 2, SEQ]), ALU.mult)

            def postnorm(n, z):
                layer, g = n // 3, 2 * (n % 3) + 1
                dve.wait_ge(s_zs, n + 1)
                link(v.reciprocal(RINV2[:, :], STD[:, :]))
                done = []

                def normal(i):
                    for t in (2 * i, 2 * i + 1):
                        ins = v.scalar_tensor_tensor(out=z[:, t, :], in0=z[:, t, :], scalar=gcol(layer, g, t),
                                                     in1=RINV2[:, :], op0=ALU.mult, op1=ALU.mult)
                    done.append(mark(ins))

                def add(i):
                    dve.wait_ge(s_dc, done[i])
                    v.tensor_tensor(pair(XF, i), pair(XF, i), pair(z, i), ALU.add).then_inc(s_xn, 1)

                normal(0)
                for i in range(1, 4):
                    normal(i)
                    add(i - 1)
                add(3)

            def convolve(layer, j):
                link(scaled(RIN[:, 2 * j:2 * j + 2, 3:], bank2(j % 3)))
                dve.sem_inc(s_evd, 1)
                if j == 0:
                    dve.wait_ge(s_bdz if layer else s_pool, 3 if layer else 15)
                for tap in range(4):
                    for t in (2 * j, 2 * j + 1):
                        w = V2[:, (layer * 4 + tap) * KT + t:(layer * 4 + tap) * KT + t + 1]
                        u = U[:, t, :]
                        r = RIN[:, t, tap:tap + SEQ]
                        if tap == 0:
                            col = 64 + layer * KT + t
                            ins = v.tensor_scalar(u, r, w, V2[:, col:col + 1], ALU.mult, ALU.add)
                        else:
                            ins = v.scalar_tensor_tensor(out=u, in0=r, scalar=w, in1=u, op0=ALU.mult, op1=ALU.add)
                    if tap < 3:
                        link(ins)
                    else:
                        ins.then_inc(s_u, 1)

            def input_gates(layer):
                dve.wait_ge(s_ga, KT * (layer + 1))
                v.tensor_tensor(IG[:, :, :], IG[:, :, :], U[:, :, :], ALU.mult).then_inc(s_iu, 1)

            def recurrence_input(layer, i):
                if i == 0:
                    dve.wait_ge(s_den, layer + 1)
                    dve.wait_ge(s_sq, layer + 1)
                    dve.wait_ge(s_iu, layer + 1)
                link(v.reciprocal(T2[:, i, :], T2[:, i, :]))
                link(v.scalar_tensor_tensor(out=SQ[:, i, :], in0=SQ[:, i, :], scalar=2.0, in1=T2[:, i, :],
                                            op0=ALU.mult, op1=ALU.mult))
                v.tensor_tensor(IG[:, i, :], IG[:, i, :], SQ[:, i, :], ALU.mult).then_inc(s_bl, 1)

            def scan(layer, g):
                dve.wait_ge(s_bl, KT * layer + 4 * g + 4)
                dve.wait_ge(s_al, 2 * layer + g + 1)
                for i in range(4 * g, 4 * g + 4):
                    ins = v.tensor_tensor_scan(RIN[:, i, 3:], T2[:, i, :], IG[:, i, :], 0.0, ALU.mult, ALU.add)
                link(ins)

            def tables_scaled(layer):
                if layer == 0:
                    dve.wait_ge(s_r1, 2)
                v.tensor_tensor(COSR[:, :], COS[:, :], RINV[:, :], ALU.mult)
                link(v.tensor_tensor(SINR[:, :], SIN[:, :], RINV[:, :], ALU.mult))

            def rotate(layer, i):
                n = 8 * layer + i
                dst = pair(Q, i) if i < 4 else pair(K, i - 4)
                cos, sin = (t[:, :].unsqueeze(1).to_broadcast([P, 2, SEQ]) for t in (COSR, SINR))
                dve.wait_ge(s_qs, n + 1)
                v.tensor_tensor(QS[:, :, :], bank2(6), sin, ALU.mult)
                link(v.tensor_tensor(dst, QT[:, i % 2, :, :], cos, ALU.mult))
                v.tensor_tensor(dst, dst, QS[:, :, :], ALU.add).then_inc(s_qr, 1)

            def mask_max(layer, h):
                n, q = HEADS * layer + h, h % 2
                dve.wait_ge(s_sc, n + 1)
                if h >= 2:
                    dve.wait_ge(s_wt, n - 1)
                for m in range(2):
                    v.tensor_tensor_reduce(SC[:, q, P * m:P * m + P], B[4 + m][:, 0:P], MASK[:, P:SEQ], 1.0,
                                           -3e38, ALU.add, ALU.max, AMX[:, q, m:m + 1])
                for m in range(2):
                    ins = v.tensor_tensor_reduce(SC[:, q, SEQ * (m + 1):SEQ * (m + 2)], B[4 + m][:, P:P + SEQ],
                                                 MASK[:, :], 1.0, -3e38, ALU.add, ALU.max, AMX[:, q, 2 + m:3 + m])
                link(ins)
                v.tensor_scalar(AMX[:, q, :], AMX[:, q, :], -HD ** -0.5, None, ALU.mult).then_inc(s_mx, 1)

            def difference(layer, h):
                n, q = HEADS * layer + h, h % 2
                dve.wait_ge(s_ex, n + 1)
                link(v.reciprocal(AR[:, q, :], ASUM[:, q, :]))
                odd = AR[:, q, :].rearrange("p (b m) -> p b m", m=2)[:, :, 1]
                v.tensor_scalar(odd, odd, NLAM[:, layer:layer + 1], None, ALU.mult)
                for b, r in ((0, SC[:, q, 0:P]), (1, SC[:, q, SEQ:2 * SEQ])):
                    ins = v.tensor_scalar(r, r, AR[:, q, 2 * b:2 * b + 1], None, ALU.mult)
                link(ins)
                v.scalar_tensor_tensor(out=SC[:, q, 0:P], in0=SC[:, q, P:2 * P], scalar=AR[:, q, 1:2],
                                       in1=SC[:, q, 0:P], op0=ALU.mult, op1=ALU.add)
                v.scalar_tensor_tensor(out=SC[:, q, SEQ:2 * SEQ], in0=SC[:, q, 2 * SEQ:3 * SEQ],
                                       scalar=AR[:, q, 3:4], in1=SC[:, q, SEQ:2 * SEQ], op0=ALU.mult,
                                       op1=ALU.add).then_inc(s_df, 1)

            def normalise_heads(layer, g):
                ms, o = (t[:, 4 * g:4 * g + 4, :] for t in (MSALL, OALL))
                dve.wait_ge(s_os, 2 * layer + g + 1)
                v.scalar_tensor_tensor(out=o, in0=o, scalar=GSUB[:, layer:layer + 1], in1=ms, op0=ALU.mult,
                                       op1=ALU.mult).then_inc(s_yf, 1)

            def split_heads(layer, g):
                dve.wait_ge(s_ybh, 2 * layer + g + 1)
                r = lambda t: t[:, 4 * g:4 * g + 4, :]
                v.tensor_tensor(r(YBL), r(OALL), r(YBH).bitcast(F32), ALU.subtract).then_inc(s_yb, 1)

            def constants():
                dve.wait_ge(s_c1, 2)
                for layer in range(DEPTH):
                    init = 0.8 - 0.6 * math.exp(-0.3 * layer)
                    link(v.tensor_tensor(NLAM[:, layer:layer + 1], SM[:, 65 + 2 * layer:66 + 2 * layer],
                                         SM[:, 64 + 2 * layer:65 + 2 * layer], ALU.subtract))
                    v.tensor_scalar(NLAM[:, layer:layer + 1], NLAM[:, layer:layer + 1], -init, None, ALU.add)
                    v.tensor_scalar(GSUB[:, layer:layer + 1], V1[:, 96 + layer:97 + layer], 1.0 - init, None, ALU.mult)
                y, s1, s2, poly = SM[:, 0:16], SM[:, 72:88], SM[:, 88:104], SM[:, 104:120]
                link(v.tensor_scalar(s1, y, 2.0, None, ALU.add))
                link(v.reciprocal(s1, s1))
                link(v.tensor_tensor(s1, s1, y, ALU.mult))
                link(v.tensor_tensor(s2, s1, s1, ALU.mult))
                link(v.tensor_scalar(poly, s2, 1.0 / 17, None, ALU.mult))
                for n in (15, 13, 11, 9, 7, 5, 3):
                    link(v.scalar_tensor_tensor(out=poly, in0=poly, scalar=1.0 / n, in1=s2, op0=ALU.add, op1=ALU.mult))
                link(v.scalar_tensor_tensor(out=poly, in0=poly, scalar=1.0, in1=s1, op0=ALU.add, op1=ALU.mult))
                link(v.scalar_tensor_tensor(out=poly, in0=poly, scalar=2.0, in1=SM[:, 32:48], op0=ALU.mult, op1=ALU.add))
                v.tensor_scalar(SPLAM[:, :], poly, 4.0, None, ALU.mult).then_inc(s_c2, 1)

            def mixer(layer):
                b = BASE[layer]
                for c in range(MIX):
                    if c == 6:
                        input_gates(layer)
                    if layer or c < MIX - 1:
                        lo(b + c + SPL)
                    if c == 0:
                        inverse(3 * layer)
                        dve.sem_inc(s_ri, 1)
                    if c < 4:
                        if c == 1 and layer == 0:
                            dve.wait_ge(s_r1, 2)
                        convolve(layer, c)
                    if c == 1 and layer == 0:
                        constants()
                    if c == 4:
                        tables_scaled(layer)
                        dve.wait_ge(s_rt, layer + 1)
                        for k in range(BLK):
                            ins = v.tensor_copy(RCOL[:, k:k + 1], B[6][:, P * k:P * k + 1])
                        ins.then_inc(s_rc, 1)
                    if 5 <= c < 13:
                        rotate(layer, c - 5)
                    if 16 <= c < 20:
                        if c == 16:
                            dve.wait_ge(s_bl, KT * (layer + 1))
                        scaled(pair(GEL, c - 16), bank2(c % 3)).then_inc(s_evd, 1)
                    if 20 <= c < 24:
                        if c == 20:
                            dve.wait_ge(s_qr, 8 * layer + 8)
                        scaled(pair(SGA, c - 20), bank2(c % 3)).then_inc(s_evd, 1)
                    if 24 <= c < 28:
                        if c == 24:
                            dve.wait_ge(s_ya, layer + 1)
                        scaled(pair(SGB, c - 24), bank2(c % 3)).then_inc(s_evd, 1)
                    if 14 <= c < 22:
                        mask_max(layer, c - 14)
                    if 15 <= c < 23:
                        difference(layer, c - 15)
                    if 8 <= c < 16:
                        recurrence_input(layer, c - 8)
                    if c in (13, 17):
                        scan(layer, (c - 13) // 4)
                    if c == 21:
                        dve.wait_ge(s_ge, layer + 1)
                        v.tensor_tensor(GEL[:, :, :], RIN[:, :, 3:], GEL[:, :, :], ALU.mult).then_inc(s_y, 1)
                    if c == 23:
                        dve.wait_ge(s_wt, HEADS * (layer + 1))
                        dve.wait_ge(s_yh, layer + 1)
                        v.tensor_tensor(YAL[:, :, :], GEL[:, :, :], YAH[:, :, :].bitcast(F32),
                                        ALU.subtract).then_inc(s_ya, 1)
                    if 28 <= c < 32:
                        i = c - 28
                        if i == 0:
                            dve.wait_ge(s_tg, 8 * layer + 8)
                        v.scalar_tensor_tensor(out=pair(SGA, i), in0=pair(SGA, i), scalar=1.0, in1=bank2(c % 3),
                                               op0=ALU.add, op1=ALU.mult).then_inc(s_evd, 1)
                    if 19 <= c < 27:
                        h = c - 19
                        dve.wait_ge(s_oe, HEADS * layer + h + 1)
                        v.reciprocal(MSALL[:, h, :], MSALL[:, h, :]).then_inc(s_or, 1)
                    if c in (28, 29):
                        normalise_heads(layer, c - 28)
                    if c in (30, 31):
                        split_heads(layer, c - 30)
                    if 32 <= c < 36:
                        i = c - 32
                        v.scalar_tensor_tensor(out=pair(SGB, i), in0=pair(SGB, i), scalar=1.0, in1=bank2(c % 3),
                                               op0=ALU.add, op1=ALU.mult).then_inc(s_evd, 1)
                        dve.wait_ge(s_evd, evd(layer, c))
                        v.tensor_tensor(pair(SGB, i), pair(SGB, i), pair(SGA, i), ALU.add).then_inc(s_m, 1)
                        dve.wait_ge(s_mh, 4 * layer + i + 1)
                        v.scalar_tensor_tensor(out=pair(YAL, i), in0=pair(SGB, i), scalar=0.5,
                                               in1=pair(YAH, i).bitcast(F32), op0=ALU.mult,
                                               op1=ALU.subtract).then_inc(s_ml, 1)

            def split_p(layer):
                dve.wait_ge(s_ph, layer + 1)
                v.tensor_tensor(PLO[:, :, :], PF[:, layer, :, :], PHI[:, :, :].bitcast(F32),
                                ALU.subtract).then_inc(s_pl, 1)

            def embed_gates(b, jobs, layer):
                for i in range(4):
                    if i:
                        dve.wait_ge(s_pe, 2 * (b + i + 1) + 2 * FFN * jobs)
                    else:
                        lo(b + i + SPL, jobs)
                        inverse(3 * layer + 2)
                        dve.wait_ge(s_pp, layer + 1)
                    scaled(PG[:, i % 2, :].rearrange("p (t s) -> p t s", t=2), bank2(4 + i)).then_inc(s_pr, 1)
                    dve.wait_ge(s_pg, 4 * layer + i + 1)
                    v.tensor_tensor(pair(Z, i), PG[:, i % 2, :].rearrange("p (t s) -> p t s", t=2), pair(PP[layer], i),
                                    ALU.mult).then_inc(s_zp, 1)
                    if i > 0 and not layer:
                        lo(b + i + SPL)

            dve.wait_ge(s_ld0, 16 * N_LD0)
            link(v.tensor_copy(POSF[:, :], POSI[:, :]))
            link(v.tensor_scalar(TT[:, 0, :], POSF[:, :], IFR[:, 0:1], None, ALU.mult))
            magic = 1.5 * 2.0 ** 23
            link(v.tensor_scalar(TT[:, 1, :], TT[:, 0, :], 1.0 / (2 * math.pi), None, ALU.mult))
            link(v.tensor_scalar(TT[:, 1, :], TT[:, 1, :], magic, None, ALU.add))
            link(v.tensor_scalar(TT[:, 1, :], TT[:, 1, :], -magic, None, ALU.add))
            c1 = 6.28125
            c2 = math.floor((2 * math.pi - c1) * 2.0 ** 20) / 2.0 ** 20
            c3 = 2 * math.pi - c1 - c2
            for c in (c1, c2, c3):
                link(v.scalar_tensor_tensor(out=TT[:, 0, :], in0=TT[:, 1, :], scalar=-c, in1=TT[:, 0, :],
                                            op0=ALU.mult, op1=ALU.add))
            link(v.tensor_scalar(TT[:, 0, :], TT[:, 0, :], 3.1415925, -3.1415925, ALU.min, ALU.max))
            link(v.scalar_tensor_tensor(out=TT[:, 2, :], in0=TT[:, 0, :], scalar=-1.0, in1=TT[:, 0, :],
                                        op0=ALU.mult, op1=ALU.max))
            v.tensor_scalar(TT[:, 1, :], TT[:, 2, :], -1.0, math.pi / 2, ALU.mult, ALU.add).then_inc(s_r0, 1)

            lo(0)
            gained(0)
            for b in range(1, SPL):
                lo(b)

            dve.wait_ge(s_tc, 2)
            dve.wait_ge(s_ld2, 16 * N_LD2)
            lam = V2[:, 112:128]
            v.scalar_tensor_tensor(out=SM[:, 16:32], in0=lam, scalar=-1.0, in1=lam, op0=ALU.mult, op1=ALU.min)
            v.tensor_scalar(SM[:, 32:48], lam, -1.0, 0.0, ALU.mult, ALU.max)
            dl = DL[:, :, :].rearrange("p (a b) d -> p a b d", b=2)
            link(v.tensor_tensor(TT[:, 3, :].rearrange("p (a d) -> p a d", a=4), dl[:, :, 0, :], dl[:, :, 1, :],
                                 ALU.mult))
            v.tensor_reduce(SM[:, 68:72], TT[:, 3, :].rearrange("p (a d) -> p a d", a=4), AX.X,
                            ALU.add).then_inc(s_c0, 1)
            mixer(0)
            postnorm(0, Z)
            gained(1)
            sum_tiles(1)
            lo(FFN0 - 1 + SPL)

            def dense(s, b, it):
                q = (b - FFN0) // 2 % 2
                fs, fa = (t[:, q, :].rearrange("p (t s) -> p t s", t=2) for t in (FS, FA))
                for n in range(2):
                    nb = b + n + SPL
                    for e in range(2):
                        dve.wait_ge(s_hi, 2 * nb + e + 1 + 24 * it)
                        r = slice(HC * e, HC * e + HC)
                        v.tensor_tensor(wlo[nb % SPL][:, r], raw[nb % RAW][:, r], whi[nb % SPL][:, r].bitcast(F32),
                                        ALU.subtract).then_inc(s_lo, 1)
                    if n == 0:
                        if isinstance(s, int) and s == 0:
                            inverse(1)
                        scaled(fs, bank2(2 * q)).then_inc(f_g, 1)
                    else:
                        ins = scaled(fa, bank2(2 * q + 1))
                ins.then_inc(f_u, 1)
                dve.wait_ge(f_u, s + 1)
                dve.wait_ge(f_s, s + 1)
                v.tensor_tensor(fa, fs, fa, ALU.mult).then_inc(f_a, 1)
                dve.wait_ge(f_h, s + 1)
                to = bass.ds(2 * s, 2) if not isinstance(s, int) else slice(2 * s, 2 * s + 2)
                v.tensor_tensor(FL[:, to, :], fa, FH[:, to, :].bitcast(F32), ALU.subtract).then_inc(f_l, 1)

            for s in range(2):
                dense(s, FFN0 + 2 * s, 0)
            with dve.Fori(0, 2) as it:
                for q in range(2, 8):
                    dense(6 * it + q, FFN0 + 2 * q, it)
            for d in range(13):
                lo(FFN0 + GU + d + SPL)
            split_p(0)
            dve.wait_ge(s_pe, 2 * (FFN0 + FFN))
            for i in range(4):
                v.tensor_copy(pair(Z, i), bank2(4 + i)).then_inc(s_zp, 1)
            dve.wait_ge(s_zp, 4)
            postnorm(1, Z)
            gained(2)
            sum_tiles(2)
            lo(FFN0 + GU + 13 + SPL)
            lo(PLE0 + SPL)
            embed_gates(PLE0 + 1, 0, 0)
            postnorm(2, Z)
            gained(3)
            mixer(1)
            split_p(1)
            postnorm(3, Z)
            dve.wait_ge(s_xs, 5)
            link(v.reciprocal(RINV[:, :], STD[:, :]))
            for t in range(KT):
                ins = v.scalar_tensor_tensor(out=HF[:, t, :], in0=XF[:, t, :], scalar=gcol(1, 2, t), in1=RINV[:, :],
                                             op0=ALU.mult, op1=ALU.mult)
                if t % 2:
                    ins.then_inc(s_hf, 1)

            def rt(n):
                return RT[:, n, :, :]

            def rt1(n):
                return RT[:, n, :, 0:1]

            def wide(n):
                return RT[:, n, :, 0:1].to_broadcast([P, BLK, EXPERTS])

            desc = SM[:, 120:136].rearrange("p (b e) -> p b e", b=BLK)
            for b in range(BLK):
                v.tensor_scalar(desc[:, b, :], IOTA[:, 0:EXPERTS], -1.0, float(EXPERTS), ALU.mult, ALU.add)
            LG, KEY, O1, O2, M1, M2, K1, W1, W2, SEL, COMB, RK, CNT, TMP = range(14)
            dve.wait_ge(r_lg, 1)
            link(v.tensor_copy(rt(LG), B[5][:, 0:2 * EXPERTS].rearrange("p (b e) -> p b e", b=BLK)))
            for one, top in ((O1, M1), (O2, M2)):
                link(v.tensor_reduce(rt1(top), rt(LG), AX.X, ALU.max))
                link(v.tensor_tensor(rt(KEY), rt(LG), wide(top), ALU.is_equal))
                link(v.tensor_tensor(rt(KEY), rt(KEY), desc, ALU.mult))
                link(v.tensor_reduce(rt1(K1), rt(KEY), AX.X, ALU.max))
                link(v.tensor_tensor(rt(one), rt(KEY), wide(K1), ALU.is_equal))
                link(v.scalar_tensor_tensor(out=rt(LG), in0=rt(one), scalar=-3e38, in1=rt(LG), op0=ALU.mult,
                                            op1=ALU.add))
            v.tensor_tensor(SM[:, 50:52].rearrange("p (b e) -> p b e", b=BLK), rt1(M2), rt1(M1),
                            ALU.subtract).then_inc(r_d, 1)
            v.tensor_tensor(rt(SEL), rt(O1), rt(O2), ALU.add).then_inc(r_sel, 1)
            def tokens_rest(n):
                dve.wait_ge(r_th, n + 1)
                r = (slice(None), n // 2, slice(512 * (n % 2), 512 * (n % 2) + 512))
                v.tensor_tensor(HTL[r[0], r[1], r[2]], B[R_BANK[n]][:, :], HTH[r[0], r[1], r[2]].bitcast(F32),
                                ALU.subtract).then_inc(r_tl, 1)
            for n in range(3):
                tokens_rest(n)
            dve.wait_ge(r_rk, 1)
            link(v.scalar_tensor_tensor(out=rt(RK), in0=B[5][:, 0:16].rearrange("p (b e) -> p b e", b=BLK),
                                        scalar=1.0, in1=rt(SEL), op0=ALU.add, op1=ALU.mult))
            link(v.tensor_scalar(JR[:, :, 0:EXPERTS], rt(RK), -1.0, None, ALU.add))

            def selection(col, sem_):
                for b in range(BLK):
                    ins = v.tensor_scalar(DSEL[:, b, :], IOTA[:, :], JR[:, b, col], None, ALU.is_equal)
                ins.then_inc(sem_, 1)

            selection(slice(0, 1), m_d)
            tokens_rest(3)
            dve.wait_ge(r_e, 1)
            ex = SM[:, 52:54].rearrange("p (b e) -> p b e", b=BLK)
            link(v.tensor_scalar(rt1(W1), ex, 1.0, None, ALU.add))
            link(v.reciprocal(rt1(W1), rt1(W1)))
            link(v.tensor_tensor(rt1(W2), rt1(W1), ex, ALU.mult))
            v.tensor_tensor(rt(COMB), rt(O1), wide(W1), ALU.mult)
            link(v.tensor_tensor(rt(TMP), rt(O2), wide(W2), ALU.mult))
            link(v.tensor_tensor(rt(COMB), rt(COMB), rt(TMP), ALU.add))
            v.tensor_copy(JC[:, :, 0:EXPERTS], rt(COMB))
            over, count, zero = RT[:, CNT, 0, :], RT[:, CNT, 1, :], RT[:, TMP, 0, :]
            v.tensor_scalar(over, B[5][:, 16:24], float(TOKENS), None, ALU.is_gt)
            link(v.memset(zero, 0.0))
            link(v.tensor_tensor_scan(count, over, zero, 0.0, ALU.add, ALU.add))
            shape = [P, MAX_EXTRA, EXPERTS]

            def each(row):
                return row.unsqueeze(1).to_broadcast(shape)

            mine, slots, weights, index = JT[:, 0], JT[:, 1:1 + BLK], JT[:, 1 + BLK:1 + 2 * BLK], JT[:, 1 + 2 * BLK]
            v.tensor_scalar(SM[:, 140:141], count[:, EXPERTS - 1:EXPERTS], float(EXPERTS), None, ALU.add)
            for e in range(MAX_EXTRA):
                ins = v.tensor_scalar(mine[:, e, :], count, e + 1.0, None, ALU.is_equal)
            link(ins)
            link(v.tensor_tensor(mine, mine, each(over), ALU.mult))
            v.tensor_tensor(index, mine, each(IOTA[:, 0:EXPERTS]), ALU.mult)
            for b in range(BLK):
                v.scalar_tensor_tensor(out=slots[:, b], in0=each(JR[:, b, 0:EXPERTS]), scalar=-float(TOKENS), in1=mine,
                                       op0=ALU.add, op1=ALU.mult)
                ins = v.tensor_tensor(weights[:, b], mine, each(RT[:, COMB, b, :]), ALU.mult)
            link(ins)
            v.tensor_reduce(SM[:, 141:141 + MAX_EXTRA], index, AX.X, ALU.add)
            v.tensor_reduce(JR[:, :, EXPERTS:EXPERTS + MAX_EXTRA], slots, AX.X, ALU.add)
            link(v.tensor_reduce(JC[:, :, EXPERTS:EXPERTS + MAX_EXTRA], weights, AX.X, ALU.add))
            v.tensor_copy(JINFO[:, :], SM[:, 140:144]).then_inc(r_j, 1)
            for u in range(2):
                dve.wait_ge(m_p7, 2 + u + 1)
                v.tensor_copy(XGL[:, 4 * u:4 * u + 4, :],
                              B[G_BANK[2 + u]][:, :].rearrange("p (t s) -> p t s", t=4)).then_inc(m_b7, 1)
            lo(PLEP1 + SPL)

            dve.wait_ge(r_j, 1)
            jobs = dve.value_load(JINFO[0:1, 0:1], min_val=EXPERTS, max_val=MAX_JOBS)
            with dve.Fori(0, jobs) as j:
                for c in range(FFN):
                    if c == FFN - 1:
                        dve.wait_ge(s_pe, 2 * (MOE0 + FFN) + 2 * FFN * j)
                        v.tensor_copy(Y[:, 512:1024], B[5][:, :]).then_inc(m_y1, 1)
                    lo(MOE0 + c + SPL, j)
                    if c < GU and c % 4 == 3:
                        f = c // 4
                        dve.wait_ge(m_s, 7 * j + f + 3)
                        v.tensor_tensor(MA[:, f % 2, :], MS[:, f % 2, :], B[2 * (f % 2) + 1][:, :],
                                        ALU.mult).then_inc(m_a, 1)
                    if c in SCATTER:
                        i = SCATTER.index(c)
                        if i == 0:
                            dve.wait_ge(m_z, 3)
                        dve.wait_ge(m_p7, 4 + U7 * j + i + 1)
                        v.tensor_tensor(pair(FACC, i), pair(FACC, i), bank2(7), ALU.add).then_inc(m_b7, 1)
                    if c % 4 == 2 and 6 <= c <= 30:
                        f = (c - 6) // 4
                        dve.wait_ge(m_th, 7 * j + f + 1)
                        v.tensor_tensor(ATL[:, 4 * f:4 * f + 4, :], B[6][:, :].rearrange("p (t s) -> p t s", t=4),
                                        ATH[:, 4 * f:4 * f + 4, :].bitcast(F32), ALU.subtract).then_inc(m_tl, 1)
                    if c == TURN_W - 3:
                        for b in range(BLK):
                            ins = v.tensor_scalar(DC[:, b, :], IOTA[:, :], JR[:, b, bass.ds(j, 1)],
                                                  JC[:, b, bass.ds(j, 1)], ALU.is_equal, ALU.mult)
                        ins.then_inc(m_dc, 1)
                    if c == TURN_W:
                        dve.wait_ge(m_p7, 4 + U7 * j + 5)
                        v.tensor_copy(S[:, :], B[7][:, 0:SEQ]).then_inc(m_b7, 1)
                    if c == 20:
                        selection(bass.ds(j + 1, 1), m_d)
                    if c in GATHER[2:]:
                        u = GATHER.index(c) - 2
                        dve.wait_ge(m_p7, 4 + U7 * j + 7 + u + 1)
                        v.tensor_copy(XGL[:, 4 * u:4 * u + 4, :],
                                      B[7][:, :].rearrange("p (t s) -> p t s", t=4)).then_inc(m_b7, 1)
            for i in range(4):
                dve.wait_ge(m_p7, 4 + U7 * jobs + i + 1)
                v.tensor_tensor(pair(FACC, i), pair(FACC, i), bank2(i), ALU.add).then_inc(s_zp, 1)
            dve.wait_ge(s_zp, 12)
            postnorm(4, FACC)
            gained(5)
            sum_tiles(5)
            embed_gates(MOE0, jobs, 1)
            postnorm(5, Z)

        @block.tensor
        def _(pe):
            mm = nc.tensor.matmul

            def three(dst, w, x, sl_w, sl_x, weights_stay, start, stop):
                wh, wl = w[0][sl_w], w[1][sl_w]
                xh, xl = x[0][sl_x], x[1][sl_x]
                terms = ((wh, xh), (wh, xl), (wl, xh)) if weights_stay else ((xh, wh), (xh, wl), (xl, wh))
                for n, (a, b) in enumerate(terms):
                    ins = mm(dst, a, b, start=start and n == 0, stop=stop and n == 2, skip_group_check=True)
                return ins

            A = slice(None)

            def wslot(b):
                return whi[b % SPL], wlo[b % SPL]

            def split(b, e, jobs=0, turns=0):
                pe.wait_ge(s_lo, 2 * b + e + 1 + 2 * FFN * jobs + 24 * turns)


            def chunk8(b, x, bank, ready=None, jobs=0, turns=0):
                for k in range(KT):
                    if k % 4 == 0:
                        split(b, k // 4, jobs, turns)
                    if ready:
                        ready(k)
                    for t in range(2):
                        ins = three(B[bank][:, SEQ * t:SEQ * t + SEQ], wslot(b), x,
                                    (A, slice(256 * k + P * t, 256 * k + P * t + P)), (A, k, A), True,
                                    k == 0 and t == 0, k == KT - 1)
                    if k % 4 == 3:
                        ins.then_inc(s_pe, 1)

            def chunk8_first(b, m, bank, jobs=0):
                n = 4 * (m if m < 4 else m - 1)
                out = [B[bank][:, SEQ * t:SEQ * t + SEQ] for t in range(2)]
                for k in range(KT):
                    if k % 4 == 0:
                        split(b, k // 4, jobs)
                    if k % 2 == 0:
                        pe.wait_ge(s_hh, n + k // 2 + 1)
                    for t in range(2):
                        cols = slice(256 * k + P * t, 256 * k + P * t + P)
                        mm(out[t], whi[b % SPL][:, cols], HH[:, k, :], start=k == 0 and t == 0, stop=False,
                           skip_group_check=True)
                        mm(out[t], wlo[b % SPL][:, cols], HH[:, k, :], start=False, stop=False, skip_group_check=True)
                for k in range(KT):
                    if k % 2 == 0:
                        pe.wait_ge(s_hl, n + k // 2 + 1)
                    for t in range(2):
                        cols = slice(256 * k + P * t, 256 * k + P * t + P)
                        ins = mm(out[t], whi[b % SPL][:, cols], HL[:, k, :], start=False, stop=k == KT - 1,
                                 skip_group_check=True)
                    if k % 4 == 3:
                        ins.then_inc(s_pe, 1)

            def chunk8v(b, x, bank):
                for k in range(KT):
                    if k % 4 == 0:
                        split(b, k // 4)
                    for t in range(BLK):
                        ins = three(B[bank][:, 256 * t:256 * t + 256], wslot(b), x,
                                    (A, slice(256 * k, 256 * k + 256)), (A, k, slice(P * t, P * t + P)), False,
                                    k == 0 and t == 0, k == KT - 1)
                    if k % 4 == 3:
                        ins.then_inc(s_pe, 1)

            def chunk2(b, x, k0, banks, first, last):
                for k in range(2):
                    chunk2_half(b, x, k0, banks, first, last, k)

            def chunk2_half(b, x, k0, banks, first, last, k):
                split(b, k)
                for t in range(KT):
                    ins = three(B[banks[t // 2]][:, SEQ * (t % 2):SEQ * (t % 2) + SEQ], wslot(b), x,
                                (A, slice(D * k + P * t, D * k + P * t + P)), (A, k0 + k, A), True,
                                first and k == 0 and t % 2 == 0, last and k == 1)
                ins.then_inc(s_pe, 1)

            def column_sum(bank, src, n, waits):
                for i in range(4):
                    waits(i)
                    for t in (2 * i, 2 * i + 1):
                        ins = mm(B[bank][:, 0:SEQ], ONES[:, :], src[:, t, :], start=t == 0, stop=t == KT - 1)
                return ins

            def sum_x(m):
                if m in BY_TILES:
                    pe.wait_ge(s_xr, BY_TILES.index(m) + 1)
                    mm(B[7][:, 0:SEQ], ONES[:, :], XSUM[:, :], start=True, stop=True).then_inc(s_xm, 1)
                    return
                column_sum(7, ZSQ, m, lambda i: pe.wait_ge(s_xq, 4 * m + i + 1)).then_inc(s_xm, 1)

            pe.wait_ge(s_pool, 15)
            pe.wait_ge(s_ldx, 32)
            for n in range(4):
                for t in (2 * n, 2 * n + 1):
                    for b in range(BLK):
                        ins = nc.tensor.transpose(B[n][:, SEQ * (t % 2) + P * b:SEQ * (t % 2) + P * b + P],
                                                  XT[:, b, P * t:P * t + P], IDENT[:, :])
                ins.then_inc(s_tp, 1)
            pe.wait_ge(s_ld1, 16 * N_LD1)
            nc.tensor.transpose(B[6][:, 0:98], R1[:, :], IDENT[0:98, 0:98])
            nc.tensor.transpose(B[6][:, 128:256], R2[:, :], IDENT[:, :]).then_inc(s_tp, 1)

            def turn_p():
                pe.wait_ge(s_ld2, 16 * N_LD2)
                for layer in range(DEPTH):
                    for k in range(PKT):
                        for b in range(BLK):
                            ins = nc.tensor.transpose(B[4 + layer][:, SEQ * k + P * b:SEQ * k + P * b + P],
                                                      PT[:, BLK * layer + b, P * k:P * k + P], IDENT[:, :])
                    ins.then_inc(s_tp, 1)

            def gate_products(layer, t):
                n = KT * layer + t
                if t % 2 == 0:
                    pe.wait_ge(s_u, 4 * layer + t // 2 + 1)
                if t == 0:
                    pe.wait_ge(s_bd, 64 * (layer + 1))
                if t >= 2:
                    pe.wait_ge(s_ga, n - 1)
                bank = B[3 if t % 2 == 0 else 7]
                for kind in range(2):
                    ins = mm(bank[:, SEQ * kind:SEQ * kind + SEQ], BD[:, kind, t, :], U[:, t, :],
                             start=True, stop=True)
                ins.then_inc(s_gt, 1)

            def swap(layer, i):
                n = 8 * layer + i
                pe.wait_ge(s_eva, eva(layer, 4 + i))
                if i:
                    pe.wait_ge(s_qr, n)
                else:
                    pe.wait_ge(s_rc, layer + 1)
                mm(B[6][:, :], SWAP[:, :], QT[:, i % 2, :, :], start=True, stop=True).then_inc(s_qs, 1)

            def scores(layer, h):
                n = HEADS * layer + h
                if h == 0:
                    pe.wait_ge(s_qr, 8 * layer + 8)
                else:
                    pe.wait_ge(s_mx, n)
                for m in range(2):
                    r = slice(HD * m, HD * m + HD)
                    mm(B[4 + m][:, 0:P], Q[r, h, 0:P], K[r, h, 0:P], start=True, stop=True)
                for m in range(2):
                    r = slice(HD * m, HD * m + HD)
                    ins = mm(B[4 + m][:, P:P + SEQ], Q[r, h, P:SEQ], K[r, h, :], start=True, stop=True)
                ins.then_inc(s_sc, 1)

            def turn(layer, h):
                n = HEADS * layer + h
                pe.wait_ge(s_df, n + 1)
                if h:
                    pe.wait_ge(s_wc, n)
                sc = SC[:, h % 2, :]
                for i, c in enumerate((0, SEQ, SEQ + P)):
                    ins = nc.tensor.transpose(B[6][:, P * i:P * i + P], sc[:, c:c + P], IDENT[:, :])
                ins.then_inc(s_wt, 1)

            def values(layer, h):
                n = HEADS * layer + h
                pe.wait_ge(s_wc, n + 1)
                if h:
                    pe.wait_ge(s_oc, n)
                else:
                    pe.wait_ge(s_eva, eva(layer, 15))
                c = slice(P * h, P * h + P)
                mm(B[7][:, 0:SEQ], V[:, 0, c], WT[:, h % 2, 0:SEQ], start=True, stop=False, skip_group_check=True)
                mm(B[7][:, P:SEQ], V[:, 1, c], WT[:, h % 2, SEQ:SEQ + P], start=False, stop=True,
                   skip_group_check=True).then_inc(s_o, 1)

            def head_square(layer, h):
                n = HEADS * layer + h
                pe.wait_ge(s_oc, n + 1)
                if h:
                    pe.wait_ge(s_oe, n)
                mm(B[3][:, 0:SEQ], ONES[:, :], OSQ[:, h % 2, :], start=True, stop=True).then_inc(s_om, 1)

            def mixer(layer):
                b = BASE[layer]
                for c in range(MIX):
                    if c >= 3:
                        if by_scalar(c - 3):
                            pe.wait_ge(s_eva, eva(layer, c - 3))
                        else:
                            pe.wait_ge(s_evd, evd(layer, c - 3))
                    bank = c % 3
                    if 12 <= c < 16:
                        chunk8v(b + c, (HH, HL), bank)
                    elif c < 28:
                        if c:
                            chunk8(b + c, (HH, HL), bank)
                        else:
                            chunk8_first(b, 3 * layer, bank)
                    elif c < 32:
                        if c == 28:
                            pe.wait_ge(s_ya, layer + 1)
                        chunk8(b + c, (YAH, YAL), bank)
                    elif c < 36:
                        ready = lambda k: pe.wait_ge(s_yb, 2 * layer + k // 4 + 1) if k % 4 == 0 else None
                        chunk8(b + c, (YBH, YBL), bank, ready if c == 32 else None)
                    else:
                        ready = lambda k: pe.wait_ge(s_ml, 4 * layer + k // 2 + 1) if k % 2 == 0 else None
                        chunk8(b + c, (YAH, YAL), bank, ready if c == 36 else None)
                    if c == 0:
                        sum_x(3 * layer)
                    if c == 1 and layer == 0:
                        turn_p()
                    if c == 2:
                        pe.wait_ge(s_ri, layer + 1)
                        for k in range(BLK):
                            ins = nc.tensor.transpose(B[6][:, P * k:P * k + P], RINV[:, P * k:P * k + P], IDENT[:, :])
                        ins.then_inc(s_rt, 1)
                    if 2 <= c < 6:
                        gate_products(layer, 2 * (c - 2))
                        gate_products(layer, 2 * (c - 2) + 1)
                    if 5 <= c < 13:
                        swap(layer, c - 5)
                    if 14 <= c < 22:
                        scores(layer, c - 14)
                    if 16 <= c < 24:
                        turn(layer, c - 16)
                    if 17 <= c < 25:
                        values(layer, c - 17)
                    if 18 <= c < 26:
                        head_square(layer, c - 18)
                column_sum(3, ZSQ, 0, lambda i: pe.wait_ge(s_eva, eva(layer, 36 + i))).then_inc(s_zm, 1)

            def sum_z_pair(z0, i, bank):
                pe.wait_ge(s_zq, z0 + i + 1)
                for t in (2 * i, 2 * i + 1):
                    ins = mm(B[bank][:, 0:SEQ], ONES[:, :], ZSQ[:, t, :], start=t == 0, stop=t == KT - 1)
                return ins

            def sum_z(z0, bank=3):
                column_sum(bank, ZSQ, 0, lambda i: pe.wait_ge(s_zq, z0 + i + 1)).then_inc(s_zm, 1)

            def embed_half(b, layer, k):
                pe.wait_ge(s_pl, layer + 1)
                chunk2_half(b, (PHI, PLO), 0, PP_BANK[layer], True, True, k)

            def embed_gates(b, jobs, layer, z0):
                for i in range(4):
                    m = 3 * layer + 2
                    if i == 3:
                        pe.wait_ge(s_xs, m + 1)
                    if i:
                        chunk8(b + i, (HH, HL), 4 + i, None, jobs)
                    else:
                        chunk8_first(b, m, 4, jobs)
                    if i == 0:
                        sum_x(m)
                pe.wait_ge(s_pp, layer + 1)
                sum_z(z0)

            mixer(0)

            def dense(s, b, it):
                q = (b - FFN0) // 2 % 2
                for n in range(2):
                    pe.wait_ge(f_a if n else f_g, s + 1)
                    first = isinstance(s, int) and s == 0 and n == 0
                    if first:
                        chunk8_first(b, 1, 0)
                        sum_x(1)
                    else:
                        chunk8(b + n, (HH, HL), 2 * q + n, None, 0, it)

            for s in range(2):
                dense(s, FFN0 + 2 * s, 0)
            with pe.Fori(0, 2) as it:
                for q in range(2, 8):
                    dense(6 * it + q, FFN0 + 2 * q, it)
            for d in range(14):
                b = FFN0 + GU + d
                pe.wait_ge(f_l, d + 1)
                chunk2(b, (FH, FL), 2 * d, (4, 5, 6, 7), d == 0, d == 13)
            embed_half(PLE0, 0, 0)
            sum_z(0, 4)
            embed_half(PLE0, 0, 1)
            embed_gates(PLE0 + 1, 0, 0, 4)
            mixer(1)
            embed_half(PLEP1, 1, 0)
            embed_half(PLEP1, 1, 1)
            sum_x(4)

            for k in range(KT):
                if k % 2 == 0:
                    pe.wait_ge(s_hf, k // 2 + 1)
                for b in range(BLK):
                    ins = mm(B[5][:, EXPERTS * b:EXPERTS * b + EXPERTS], HF[:, k, P * b:P * b + P], RW[:, k, :],
                             start=k == 0 and b == 0, stop=k == KT - 1, skip_group_check=True)
            ins.then_inc(r_lg, 1)
            def ranks():
                pe.wait_ge(r_sel, 1)
                sel = (RT[:, 9, 0, :], RT[:, 9, 1, :])
                mm(B[5][:, 0:8], BEFORE[:, :], sel[0], start=True, stop=True)
                mm(B[5][:, 8:16], ONES[:, :], sel[0], start=True, stop=False)
                mm(B[5][:, 8:16], BEFORE[:, :], sel[1], start=False, stop=True)
                mm(B[5][:, 16:24], ONES[:, :], sel[0], start=True, stop=False)
                mm(B[5][:, 16:24], ONES[:, :], sel[1], start=False, stop=True).then_inc(r_rk, 1)

            for n in range(4):
                if n == 3:
                    ranks()
                    pe.wait_ge(r_tl, 1)
                for t in range(4):
                    ins = nc.tensor.transpose(B[R_BANK[n]][:, P * t:P * t + P],
                                              HF[:, 4 * (n % 2) + t, P * (n // 2):P * (n // 2) + P], IDENT[:, :])
                ins.then_inc(r_tp, 1)
            def gather(u, bank=7):
                src = HTH if u < 2 else HTL
                for i in range(4):
                    t = 4 * (u % 2) + i
                    for b in range(BLK):
                        ins = mm(B[bank][:, P * i:P * i + P], src[:, b, P * t:P * t + P], DSEL[:, b, :],
                                 start=b == 0, stop=b == BLK - 1)
                ins.then_inc(m_p7, 1)

            def scatter(i, bank):
                for t in (2 * i, 2 * i + 1):
                    ins = mm(B[bank][:, SEQ * (t % 2):SEQ * (t % 2) + SEQ], Y[:, P * t:P * t + P], S[:, :],
                             start=True, stop=True)
                ins.then_inc(m_p7, 1)

            pe.wait_ge(m_d, 1)
            for u in range(4):
                if u == 0:
                    pe.wait_ge(r_th, 4)
                if u == 1:
                    pe.wait_ge(r_tl, 4)
                if u == 3:
                    pe.wait_ge(m_b7, 3)
                gather(u, G_BANK[u])
            pe.wait_ge(s_pp, DEPTH)
            pe.wait_ge(m_z, 3)
            pe.wait_ge(r_j, 1)
            jobs = pe.value_load(JINFO[0:1, 0:1], min_val=EXPERTS, max_val=MAX_JOBS)
            with pe.Fori(0, jobs) as j:
                for c in range(FFN):
                    b = MOE0 + c
                    if c == 0:
                        pe.wait_ge(m_b7, 4 + U7 * j)
                    if c < GU:
                        f, part = c // 4, c % 4
                        bank = 2 * (f % 2) + part // 2
                        if part % 2 == 0:
                            pe.wait_ge(m_a if part else m_s, 7 * j + (f + 1 if f else 2))
                        for k in range(4):
                            kt = 4 * (part % 2) + k
                            if k % 2 == 0:
                                split(b, k // 2, j)
                            ins = three(B[bank][:, :], wslot(b), (XGH, XGL), (A, slice(512 * k, 512 * k + 512)),
                                        (A, kt, A), False, kt == 0, kt == KT - 1)
                            if k % 2 == 1:
                                ins.then_inc(s_pe, 1)
                    else:
                        d = c - GU
                        if d == 0:
                            pe.wait_ge(m_y0, j + 1)
                            pe.wait_ge(m_y1, j + 1)
                        if d % 2 == 0:
                            pe.wait_ge(m_tl, 7 * j + 2 + d // 2)
                        for k in range(2):
                            split(b, k, j)
                            for h in range(2):
                                ins = three(B[4 + h][:, :], wslot(b), (ATH, ATL),
                                            (A, slice(D * k + 512 * h, D * k + 512 * h + 512)), (A, 2 * d + k, A),
                                            False, d == 0 and k == 0, d == 13 and k == 1)
                            ins.then_inc(s_pe, 1)
                    if c in SCATTER:
                        i = SCATTER.index(c)
                        if i == 0:
                            pe.wait_ge(m_y0, j + 1)
                            pe.wait_ge(m_y1, j + 1)
                        pe.wait_ge(m_b7, 4 + U7 * j + i)
                        scatter(i, 7)
                    if c % 4 == 1 and 5 <= c < 30:
                        f = (c - 5) // 4
                        pe.wait_ge(m_a, 7 * j + f + 3)
                        pe.wait_ge(m_tl, 7 * j + f + 1)
                        for i in range(4):
                            ins = nc.tensor.transpose(B[6][:, P * i:P * i + P], MA[:, f % 2, P * i:P * i + P],
                                                      IDENT[:, :])
                        ins.then_inc(m_t, 1)
                    if c == TURN_W:
                        pe.wait_ge(m_dc, j + 1)
                        pe.wait_ge(m_b7, 4 + U7 * j + 4)
                        for t in range(BLK):
                            ins = nc.tensor.transpose(B[7][:, P * t:P * t + P], DC[:, t, :], IDENT[:, :])
                        ins.then_inc(m_p7, 1)
                    if c in GATHER:
                        u = GATHER.index(c)
                        pe.wait_ge(m_d, j + 2)
                        pe.wait_ge(m_b7, 4 + U7 * j + 5 + u)
                        gather(u)
            pe.wait_ge(m_y0, jobs + 1)
            pe.wait_ge(m_y1, jobs + 1)
            pe.wait_ge(m_b7, 4 + U7 * jobs)
            for i in range(4):
                scatter(i, i)
                if i:
                    sum_z_pair(8, i - 1, 4)
            sum_z_pair(8, 3, 4).then_inc(s_zm, 1)
            embed_gates(MOE0, jobs, 1, 12)
            for n in range(4):
                for t in range(4):
                    k = 4 * (n % 2) + t
                    pe.wait_ge(s_xn, 24 + k // 2 + 1)
                    ins = nc.tensor.transpose(B[n][:, P * t:P * t + P],
                                              XF[:, k, P * (n // 2):P * (n // 2) + P], IDENT[:, :])
                ins.then_inc(s_ot, 1)


_INS = ['x', 'p', 'positions', 'norm_g', 'w_in', 'conv_w', 'conv_b', 'lru_wa', 'lru_ba', 'lru_wx', 'lru_bx', 'lru_lam',
        'diff_lambda', 'subln_g', 'w_proj_a', 'w_proj_b', 'w_out', 'ffn_w_gate', 'ffn_w_up', 'ffn_w_down', 'router_w',
        'moe_w_gate', 'moe_w_up', 'moe_w_down', 'ple_w_proj', 'ple_w_gate']


def kernel(**inputs):
    import numpy as _np
    import concourse.bacc as _bacc
    from concourse import mybir as _mybir
    from concourse.bass_utils import run_bass_kernel_spmd as _run

    nc = _bacc.Bacc("TRN2", target_bir_lowering=False, num_devices=1)
    given = {name: _np.ascontiguousarray(inputs[name]) for name in _INS}
    freq = 10000.0 ** (-_np.arange(0, HD, 2, dtype=_np.float64) / HD)
    given['inv_freq'] = _np.tile(freq.astype(_np.float32), 4).reshape(P, 1)
    arrays, args = {}, []
    for name, a in given.items():
        arrays[f"in_{name}_dram"] = a
        args.append(nc.dram_tensor(f"in_{name}_dram", a.shape, _mybir.dt.from_np(a.dtype), kind="ExternalInput").ap())
    args.append(nc.dram_tensor("out_0_dram", (1, SEQ, D), F32, kind="ExternalOutput").ap())
    bass_hybrid_rglru_diffattn_moe(nc, *args)
    r = _run(nc, [arrays], core_ids=[0])
    return r.results[0]["out_0_dram"]
```
